# Optimizing a Trainium2 kernel written in Bass

```python
import math
import jax
import jax.numpy as jnp
from jax import lax
import numpy as np

D_MODEL = 2048
BATCH = 1
SEQ = 256
DEPTH = 2

CHUNK = 64
Q_BLOCK = 128
N_MIXERS = 2
RMS_EPS = 1e-6
NEG_INF = -1e30

MLA_HEADS = 16
MLA_Q_RANK = 512
MLA_KV_RANK = 512
MLA_NOPE = 128
MLA_ROPE = 64
MLA_V = 128
MLA_QK = MLA_NOPE + MLA_ROPE
MLA_IN = MLA_Q_RANK + MLA_KV_RANK + MLA_ROPE
ROPE_THETA = 10000.0

FOX_HEADS = 16
FOX_HEAD_DIM = D_MODEL // FOX_HEADS
FOX_IN = 4 * D_MODEL + FOX_HEADS

PEER_HEADS = 8
PEER_N_KEYS = 128
PEER_N_EXPERTS = PEER_N_KEYS * PEER_N_KEYS
PEER_D_KEY = 256
PEER_D_HALF = PEER_D_KEY // 2
PEER_TOPK = 16
PEER_TOKEN_BLOCK = 128

kernel_name = 'hybrid_mla_fox_peer_streaming_encoder'

def rms_norm(x, g):
    xf = x.astype(jnp.float32)
    y = xf * lax.rsqrt(jnp.mean(xf * xf, axis=-1, keepdims=True) + RMS_EPS)
    return (y * g.astype(jnp.float32)).astype(x.dtype)

def rotate(x, cos, sin):
    x1, x2 = jnp.split(x, 2, axis=-1)
    return jnp.concatenate([x1 * cos - x2 * sin, x2 * cos + x1 * sin], axis=-1)

def blocked_attention(q, k, v, scale, chunk_causal, log_decay=None):
    seq = q.shape[1]
    outs = []
    for qb in range(seq // Q_BLOCK):
        q0 = qb * Q_BLOCK
        q1 = q0 + Q_BLOCK
        logits = jnp.einsum('bqhd,bkhd->bhqk', q[:, q0:q1], k[:, :q1]).astype(jnp.float32) * scale
        t = jnp.arange(q0, q1)[:, None]
        s = jnp.arange(q1)[None, :]
        if chunk_causal:
            allowed = (s // CHUNK) <= (t // CHUNK)
        else:
            allowed = s <= t
        if log_decay is not None:
            logits = logits + (log_decay[:, :, q0:q1, None] - log_decay[:, :, None, :q1])
        logits = jnp.where(allowed, logits, NEG_INF)
        p = jax.nn.softmax(logits, axis=-1).astype(v.dtype)
        outs.append(jnp.einsum('bhqk,bkhd->bqhd', p, v[:, :q1]))
    return jnp.concatenate(outs, axis=1)

def mla_mixer(h, cos, sin, w_in, g_qa, w_qb, g_kva, w_kvb, g_q, g_k, w_o):
    b, s, _ = h.shape
    z = h @ w_in
    c_q, c_kv, k_rope = jnp.split(z, [MLA_Q_RANK, MLA_Q_RANK + MLA_KV_RANK], axis=-1)
    q = (rms_norm(c_q, g_qa) @ w_qb).reshape(b, s, MLA_HEADS, MLA_QK)
    kv = (rms_norm(c_kv, g_kva) @ w_kvb).reshape(b, s, MLA_HEADS, MLA_NOPE + MLA_V)
    k_nope, v = jnp.split(kv, [MLA_NOPE], axis=-1)
    k_rope = jnp.broadcast_to(k_rope[:, :, None, :], (b, s, MLA_HEADS, MLA_ROPE))
    k = jnp.concatenate([k_nope, k_rope], axis=-1)
    q = rms_norm(q, g_q)
    k = rms_norm(k, g_k)
    q = jnp.concatenate([q[..., :MLA_NOPE], rotate(q[..., MLA_NOPE:], cos, sin)], axis=-1)
    k = jnp.concatenate([k[..., :MLA_NOPE], rotate(k[..., MLA_NOPE:], cos, sin)], axis=-1)
    o = blocked_attention(q, k, v, 1.0 / math.sqrt(MLA_QK), chunk_causal=True)
    return o.reshape(b, s, MLA_HEADS * MLA_V) @ w_o

def fox_mixer(h, w_in, b_f, g_q, g_k, w_o):
    b, s, _ = h.shape
    z = h @ w_in
    q, k, v, gate, f_logit = jnp.split(z, [D_MODEL, 2 * D_MODEL, 3 * D_MODEL, 4 * D_MODEL], axis=-1)
    q = rms_norm(q.reshape(b, s, FOX_HEADS, FOX_HEAD_DIM), g_q)
    k = rms_norm(k.reshape(b, s, FOX_HEADS, FOX_HEAD_DIM), g_k)
    v = v.reshape(b, s, FOX_HEADS, FOX_HEAD_DIM)
    log_f = jax.nn.log_sigmoid((f_logit + b_f).astype(jnp.float32))
    c = jnp.cumsum(log_f, axis=1).transpose(0, 2, 1)
    o = blocked_attention(q, k, v, 1.0 / math.sqrt(FOX_HEAD_DIM), chunk_causal=False, log_decay=c)
    o = o.reshape(b, s, D_MODEL) * jax.nn.sigmoid(gate)
    return o @ w_o

def peer_ffn(h, w_q, sub_keys, u, v):
    b, s, d = h.shape
    t = b * s
    x = h.reshape(t, d)
    q = (x @ w_q).reshape(t, PEER_HEADS, 2, PEER_D_HALF)
    scores = jnp.einsum('thcd,cnd->thcn', q, sub_keys).astype(jnp.float32)
    top_s, top_i = lax.top_k(scores, PEER_TOPK)
    cand_s = top_s[..., 0, :, None] + top_s[..., 1, None, :]
    cand_i = top_i[..., 0, :, None] * PEER_N_KEYS + top_i[..., 1, None, :]
    cand_s = cand_s.reshape(t, PEER_HEADS, PEER_TOPK * PEER_TOPK)
    cand_i = cand_i.reshape(t, PEER_HEADS, PEER_TOPK * PEER_TOPK)
    best_s, pos = lax.top_k(cand_s, PEER_TOPK)
    idx = jnp.take_along_axis(cand_i, pos, axis=-1)
    g = jax.nn.softmax(best_s, axis=-1).astype(h.dtype)
    n_sel = PEER_HEADS * PEER_TOPK
    n_blk = t // PEER_TOKEN_BLOCK
    xb = x.reshape(n_blk, PEER_TOKEN_BLOCK, d)
    ib = idx.reshape(n_blk, PEER_TOKEN_BLOCK, n_sel)
    gb = g.reshape(n_blk, PEER_TOKEN_BLOCK, n_sel)

    def one_block(args):
        x_blk, i_blk, g_blk = args
        u_sel = u[i_blk]
        a = jax.nn.gelu(jnp.einsum('tkd,td->tk', u_sel, x_blk), approximate=False) * g_blk
        return jnp.einsum('tk,tkd->td', a, v[i_blk])

    out = lax.map(one_block, (xb, ib, gb))
    return out.reshape(b, s, d)

def setup_inputs(seed: int = 0) -> dict:
    key = jax.random.key(seed)
    ks = jax.random.split(key, 24)
    f32 = jnp.float32
    n_a = (DEPTH + N_MIXERS - 1) // N_MIXERS
    n_b = DEPTH // N_MIXERS

    def nrm(k, shape, scale):
        return jax.random.normal(k, shape, f32) * scale

    def gain(k, shape):
        return 1.0 + 0.02 * jax.random.normal(k, shape, f32)

    x = jax.random.normal(ks[0], (BATCH, SEQ, D_MODEL), f32)
    start = jax.random.randint(ks[1], (BATCH, 1), 0, 8 * SEQ, dtype=jnp.int32)
    positions = (start + jnp.arange(SEQ, dtype=jnp.int32)[None, :]).astype(jnp.int32)
    fox_b_f = jnp.linspace(1.0, 6.0, FOX_HEADS, dtype=f32)[None, :] + 0.1 * jax.random.normal(ks[15], (n_b, FOX_HEADS), f32)
    return {
        'x': x,
        'positions': positions,
        'norm_mix_g': gain(ks[2], (DEPTH, D_MODEL)),
        'norm_ffn_g': gain(ks[3], (DEPTH, D_MODEL)),
        'mla_w_in': nrm(ks[4], (n_a, D_MODEL, MLA_IN), D_MODEL ** -0.5),
        'mla_g_qa': gain(ks[5], (n_a, MLA_Q_RANK)),
        'mla_w_qb': nrm(ks[6], (n_a, MLA_Q_RANK, MLA_HEADS * MLA_QK), MLA_Q_RANK ** -0.5),
        'mla_g_kva': gain(ks[7], (n_a, MLA_KV_RANK)),
        'mla_w_kvb': nrm(ks[8], (n_a, MLA_KV_RANK, MLA_HEADS * (MLA_NOPE + MLA_V)), MLA_KV_RANK ** -0.5),
        'mla_g_q': gain(ks[9], (n_a, MLA_QK)),
        'mla_g_k': gain(ks[10], (n_a, MLA_QK)),
        'mla_w_o': nrm(ks[11], (n_a, MLA_HEADS * MLA_V, D_MODEL), (MLA_HEADS * MLA_V) ** -0.5),
        'fox_w_in': nrm(ks[12], (n_b, D_MODEL, FOX_IN), D_MODEL ** -0.5),
        'fox_b_f': fox_b_f,
        'fox_g_q': gain(ks[13], (n_b, FOX_HEAD_DIM)),
        'fox_g_k': gain(ks[14], (n_b, FOX_HEAD_DIM)),
        'fox_w_o': nrm(ks[16], (n_b, D_MODEL, D_MODEL), D_MODEL ** -0.5),
        'peer_w_q': nrm(ks[17], (DEPTH, D_MODEL, PEER_HEADS * PEER_D_KEY), D_MODEL ** -0.5),
        'peer_sub_keys': nrm(ks[18], (DEPTH, 2, PEER_N_KEYS, PEER_D_HALF), PEER_D_HALF ** -0.5),
        'peer_u': nrm(ks[19], (DEPTH, PEER_N_EXPERTS, D_MODEL), D_MODEL ** -0.5),
        'peer_v': nrm(ks[20], (DEPTH, PEER_N_EXPERTS, D_MODEL), PEER_HEADS ** -0.5),
    }

def reference(x, positions, norm_mix_g, norm_ffn_g, mla_w_in, mla_g_qa, mla_w_qb, mla_g_kva, mla_w_kvb, mla_g_q, mla_g_k, mla_w_o, fox_w_in, fox_b_f, fox_g_q, fox_g_k, fox_w_o, peer_w_q, peer_sub_keys, peer_u, peer_v):
    inv_freq = ROPE_THETA ** (-jnp.arange(0, MLA_ROPE, 2, dtype=jnp.float32) / MLA_ROPE)
    ang = positions.astype(jnp.float32)[..., None] * inv_freq
    cos = jnp.cos(ang)[:, :, None, :].astype(x.dtype)
    sin = jnp.sin(ang)[:, :, None, :].astype(x.dtype)
    for i in range(DEPTH):
        j = i // N_MIXERS
        h = rms_norm(x, norm_mix_g[i])
        if i % N_MIXERS == 0:
            y = mla_mixer(h, cos, sin, mla_w_in[j], mla_g_qa[j], mla_w_qb[j], mla_g_kva[j], mla_w_kvb[j], mla_g_q[j], mla_g_k[j], mla_w_o[j])
        else:
            y = fox_mixer(h, fox_w_in[j], fox_b_f[j], fox_g_q[j], fox_g_k[j], fox_w_o[j])
        x = x + y
        h = rms_norm(x, norm_ffn_g[i])
        x = x + peer_ffn(h, peer_w_q[i], peer_sub_keys[i], peer_u[i], peer_v[i])
    return x


_drawn_inputs = setup_inputs


def setup_inputs(seed=0):
    import zlib

    import numpy as np

    out = dict(_drawn_inputs(seed))
    spreads = {}
    factors = {'mla_g_qa': 2.809, 'mla_g_q': 2.806, 'mla_g_k': 2.916, 'fox_g_q': 5.53, 'fox_g_k': 5.787}
    for name, (base, spread) in spreads.items():
        noise = np.random.default_rng([zlib.crc32(name.encode()), seed]).standard_normal(out[name].shape)
        drawn = base * np.exp(spread * noise) if base else spread * noise
        out[name] = jnp.asarray(drawn.astype(out[name].dtype))
    for name, factor in factors.items():
        out[name] = (out[name] * factor).astype(out[name].dtype)
    return out
```

```python
from contextlib import ExitStack

import numpy as np

import concourse.bass as bass
from concourse import mybir

ALU = mybir.AluOpType
ACT = mybir.ActivationFunctionType
AX_X = mybir.AxisListType.X
F32 = mybir.dt.float32
I32 = mybir.dt.int32
U32 = mybir.dt.uint32

P = 128
NB = 2
T = NB * P
D = 2048
KC = D // P
TILE = 512
CHUNK = 64
EPS = 1e-6
MASKED = -1e30
LOWEST = -3.0e38

Q_RANK = KV_RANK = 512
RC = Q_RANK // P
NOPE, ROPE, VDIM = 128, 64, 128
HALF = ROPE // 2
MLA_QK = NOPE + ROPE
HEADS = 16
HD = 128
PHEADS, KEYS, TOPK = 8, 128, 16
RING = 4
SLOTS = TOPK

TWO_PI = 6.283185307179586
ROUND_MAGIC = 12582912.0
PI_A, PI_B, PI_C = 6.28125, 1.93500518798828125e-3, 3.0199159819567e-7
PI_SAFE = 3.1415925
ROPE_THETA = 10000.0
MATCH_AT = 8
CHOOSE_AT = 11
CHOOSE_STEPS = 24


class Events:

    def __init__(self, sem, n):
        self.sem, self.n = sem, n

    def credit(self, eng):
        eng.sem_inc(self.sem, self.n)

    def at(self, turn, event):
        return (turn + 1) * self.n + event + 1

    def done(self, eng, turn, event, back=0):
        eng.wait_ge(self.sem, self.at(turn, event) - back)

    def turn_before(self, eng, turn, event=None):
        eng.wait_ge(self.sem, self.at(turn, self.n - 1 if event is None else event) - self.n)


class Chain:

    def __init__(self, eng, sem):
        self.eng, self.sem, self.base, self.n = eng, sem, 0, 0

    def step(self, ins):
        ins.then_inc(self.sem, 1)
        self.n += 1

    def settle(self):
        self.eng.wait_ge(self.sem, self.base + self.n)

    def enter(self, i, per):
        self.outer, self.per = self.base + self.n, per
        self.base, self.n = self.outer + i * per, 0

    def leave(self, turns):
        assert self.n == self.per, (self.n, self.per)
        self.base, self.n = self.outer + turns * self.per, 0


def rows_view(w):
    return w.rearrange("(k p) n -> p k n", p=P)


def hybrid_encoder(nc, x, positions, norm_mix_g, norm_ffn_g, mla_w_in, mla_g_qa, mla_w_qb, mla_g_kva,
                   mla_w_kvb, mla_g_q, mla_g_k, mla_w_o, fox_w_in, fox_b_f, fox_g_q, fox_g_k, fox_w_o,
                   peer_w_q, peer_sub_keys, peer_u, peer_v, inv_freq, out):
    with ExitStack() as ctx:
        def sb(name, shape, dt=F32):
            return ctx.enter_context(nc.sbuf_tensor(name, shape, dt))

        def sem(name):
            return ctx.enter_context(nc.semaphore(name))

        resid = sb("resid", [P, NB, D])
        normed = sb("normed", [P, NB, D])
        normedT = sb("normedT", [P, KC, T])
        share = sb("share", [P, NB * D])
        attnT = share[:, :].rearrange("p (k t) -> p k t", k=KC)
        wbuf = sb("wbuf", [P, 2, KC, TILE])
        room = sb("room", [P, 2 * RING * D])
        u_ring = room[:, 0:RING * D].rearrange("p (r d) -> p r d", r=RING)
        v_ring = room[:, RING * D:2 * RING * D].rearrange("p (r d) -> p r d", r=RING)

        taken = [0]

        def area(n, **dims):
            a = room[:, taken[0]:taken[0] + n]
            taken[0] += n
            if dims:
                names = list(dims)
                a = a.rearrange(f"p ({' '.join(names)} rest) -> p {' '.join(names)} rest", **dims)
            return a

        gain_row = area(D)
        squares = area(NB * D, b=NB)
        taken[0] = 0
        raw_q = area(NB * TILE, b=NB)
        raw_k = area(NB * TILE, b=NB)
        raw_v = area(NB * TILE, b=NB)
        qn = area(NB * TILE, b=NB)
        kn = area(NB * TILE, b=NB)
        gate = area(NB * TILE, b=NB)
        qT = area(4 * T, h=4)
        kT = area(4 * T, h=4)
        qropeT = area(T)
        kropeT = area(T)
        masked = area(2 * T, r=2)
        probs = area(2 * T, r=2)
        probsT = area(2 * T, r=2, k=NB)
        og = area(2 * P, r=2)
        tmp_a = area(NB * 2 * ROPE, b=NB, h=2)
        tmp_b = area(NB * 2 * ROPE, b=NB, h=2)
        cqT = area(RC * T, c=RC)
        ckvT = area(RC * T, c=RC)
        taken[0] -= 2 * RC * T
        decay_rows = area(HEADS * T, h=HEADS)
        fl = area(5 * NB * HEADS, m=5, b=NB)
        decayT = area(T)
        assert taken[0] <= 2 * RING * D
        scores = share[:, 0:D]
        peer_qT = share[:, D:D + 2 * T].rearrange("p (c t) -> p c t", c=2)

        ident = sb("ident", [P, P])
        mask_mla = sb("mask_mla", [P, T])
        mask_fox = sb("mask_fox", [P, T])
        upto = sb("upto", [P, T])
        iota = sb("iota", [P, TOPK])
        inv_row = sb("inv_row", [P, HALF])
        pos_i = sb("pos_i", [P, NB], I32)
        pos_f = sb("pos_f", [P, NB])
        cos2 = sb("cos2", [P, NB, ROPE])
        sin2 = sb("sin2", [P, NB, ROPE])
        g_qa, g_kva = share[:, 0:Q_RANK], share[:, Q_RANK:Q_RANK + KV_RANK]
        keys_n = share[:, 1024:1024 + 4 * P].rearrange("p (m d) -> p m d", m=4)
        ang = share[:, 1536:1536 + 4 * T // 4].rearrange("p (m b f) -> p m b f", m=4, b=NB)
        g_cols = sb("g_cols", [P, 4])
        g_qrope = sb("g_qrope", [P, ROPE])
        g_krope = sb("g_krope", [P, ROPE])
        b_f = sb("b_f", [P, HEADS])
        k_rot = sb("k_rot", [P, NB, ROPE])
        keysT = sb("keysT", [P, 4, KEYS])
        stat = sb("stat", [P, 96])
        n_sum, n_root, n_inv = stat[:, 0:2], stat[:, 2:4], stat[:, 4:6]
        h_sum, h_root, h_inv = stat[:, 8:16], stat[:, 16:24], stat[:, 24:32]
        row_max, neg_max, row_sum, inv_sum = (stat[:, 32 + 8 * i:40 + 8 * i] for i in range(4))
        rope_sum = stat[:, 64:66]
        l_sum, l_root, l_inv = stat[:, 68:72], stat[:, 72:76], stat[:, 76:80]
        k_sum, k_root, k_inv = stat[:, 80:84], stat[:, 84:88], stat[:, 88:92]

        pick = sb("pick", [P, 2, KEYS])
        work = sb("work", [P, 2 * TOPK, TOPK])
        work_flat = work[:, :, :].rearrange("p a b -> p (a b)")
        pick_flat = pick[:, :, :].rearrange("p c n -> p (c n)")
        pick2 = work_flat[:, 0:2 * KEYS].rearrange("p (c n) -> p c n", c=2)
        cand2 = work_flat[:, 2 * KEYS:4 * KEYS]
        onehot = work
        top_s = sb("top_s", [P, 2, TOPK])
        top_i = sb("top_i", [P, 2, TOPK], U32)
        top_if = sb("top_if", [P, 2, TOPK])
        cand = sb("cand", [P, TOPK * TOPK])
        best = sb("best", [P, TOPK])
        best_pos = sb("best_pos", [P, TOPK], U32)
        pair = sb("pair", [P, 2, TOPK], U32)
        pair_f = sb("pair_f", [P, 2 * TOPK])
        key_f = sb("key_f", [P, 2 * TOPK])
        soft = sb("soft", [P, 4])
        soft_e = sb("soft_e", [P, TOPK])
        gates = sb("gates", [P, 2, TOPK])
        index = sb("index", [P, 2, TOPK], U32)
        dots = sb("dots", [P, RING])
        acts = sb("acts", [P, 2, RING])
        diag = sb("diag", [P, RING, P])

        psum = ctx.enter_context(nc.psum_tensor("psum", [P, 8, TILE], F32))

        def gbank(half, b):
            return psum[:, 2 * half + b, :]

        def sbank(r):
            return psum[:, 4 + r, :]

        def pt_bank(r):
            return psum[:, 6 + r, 0:T].rearrange("p (k t) -> p k t", k=NB)

        def o_bank(r):
            return psum[:, r, 0:P]

        def ot_bank(r):
            return psum[:, 2 + r, 0:P]

        consts_made = sem("consts_made")
        x_loaded = sem("x_loaded")
        small_loaded = sem("small_loaded")
        gains_loaded = sem("gains_loaded")
        held = {e: sem(f"held_{e}") for e in ("pool", "dve", "act")}
        dve_steps, act_steps = sem("dve_steps"), sem("act_steps")
        w_full = [sem(f"w_full{i}") for i in range(2)]
        w_used = [sem(f"w_used{i}") for i in range(2)]
        g_full = [sem(f"g_full{i}") for i in range(2)]
        evac = [sem(f"evac{i}") for i in range(2)]
        norm_root, norm_done = sem("norm_root"), sem("norm_done")
        ht_full, ht_done = sem("ht_full"), sem("ht_done")
        keys_full, keys_done = sem("keys_full"), sem("keys_done")
        angles_ready, trig_ready = sem("angles_ready"), sem("trig_ready")
        lat_ss, lat_root, lat_norm, lat_full, lat_done = (
            sem(n) for n in ("lat_ss", "lat_root", "lat_norm", "lat_full", "lat_done"))
        forget_in, forget_ln, forget_log, decay_full, decay_ready = (
            sem(n) for n in ("forget_in", "forget_ln", "forget_log", "decay_full", "decay_ready"))
        o_added = sem("o_added")
        query_full, query_done, match_full, match_done = (
            sem(n) for n in ("query_full", "query_done", "match_full", "match_done"))
        acc_zero = sem("acc_zero")
        pick_ready, pick_used = sem("pick_ready"), sem("pick_used")
        best_ready, exp_ready, gate_ready, index_ready = (
            sem(n) for n in ("best_ready", "exp_ready", "gate_ready", "index_ready"))
        u_full = [sem(f"u_full{r}") for r in range(RING)]
        v_full = [sem(f"v_full{r}") for r in range(RING)]
        dot_done, diag_ready, mm_done = sem("dot_done"), sem("diag_ready"), sem("mm_done")
        peer_added = sem("peer_added")
        stored = sem("stored")

        class Attn:

            def __init__(self, layer, nh, tiles, w0, g0):
                self.layer, self.nh, self.tiles = layer, nh, tiles
                self.groups = HEADS // nh
                self.w0, self.g0 = w0, g0
                self.fox = layer == 1
                self.jobs = [(h, b) for h in range(nh) for b in range(NB)]
                nj = len(self.jobs)

                def ev(name, n):
                    return Events(sem(f"{name}{layer}"), n)

                self.ss_ready = ev("ss_ready", 2)
                self.root_ready = ev("root_ready", 2)
                self.qk_norm = ev("qk_norm", 4)
                self.t_full = ev("t_full", 4)
                self.t_done = ev("t_done", 4)
                self.s_full = ev("s_full", nj)
                self.masked = ev("masked", nj)
                self.negated = ev("negated", nj)
                self.exped = ev("exped", nj)
                self.pt_full = ev("pt_full", nj)
                self.pt_done = ev("pt_done", nj)
                self.o_full = ev("o_full", nj)
                self.og_done = ev("og_done", nj)
                self.ot_full = ev("ot_full", nj)
                self.ot_done = ev("ot_done", nj)

            def turn(self, n0, g, t):
                return (n0 + t) % 2, (n0 + t) // 2 + (self.tiles // 2) * g

            def w(self, g, t):
                return self.turn(self.w0, g, t)

            def g(self, g, t):
                return self.turn(self.g0, g, t)

        W_IN = 0
        W_MLA = W_IN + 3
        W_O0 = W_MLA + 2 * 8
        W_PQ0 = W_O0 + 4
        W_F = W_PQ0 + PHEADS
        W_FOX = W_F + 1
        W_O1 = W_FOX + 4 * 4
        W_PQ1 = W_O1 + 4
        G_IN = 0
        G_MLA = G_IN + 3
        G_O0 = G_MLA + 2 * 8
        G_F = G_O0 + 4
        G_FOX = G_F + 1
        G_O1 = G_FOX + 4 * 4
        W_O, W_PQ, G_O = (W_O0, W_O1), (W_PQ0, W_PQ1), (G_O0, G_O1)
        mla = Attn(0, 2, 2, W_MLA, G_MLA)
        fox = Attn(1, 4, 4, W_FOX, G_FOX)
        layers = (mla, fox)

        N_CONST = 9
        N_SMALL = 13
        block = ctx.enter_context(nc.Block())

        @block.sync
        def _(sp):
            def load_tile(half, number, parts):
                sp.wait_ge(w_used[half], number + 1)
                assert len(parts) == 4
                for dst, src in parts:
                    sp.dma_start(dst, src).then_inc(w_full[half], 16)

            def quarters(half, w, cols, n):
                step = w.shape[1] // 4
                return [(wbuf[:, half, q * step:(q + 1) * step, 0:n], w[:, q * step:(q + 1) * step, cols])
                        for q in range(4)]

            def load_gains(p, g):
                sp.dma_start(gain_row, g.broadcast_to([P, D])).then_inc(gains_loaded, 16)

            for b in range(NB):
                sp.dma_start(resid[:, b, :], x[0, b * P:(b + 1) * P, :]).then_inc(x_loaded, 16)
            load_gains(0, norm_mix_g[0:1, :])
            w_in = rows_view(mla_w_in[0])
            widths = (Q_RANK, KV_RANK, ROPE)
            for t in range(3):
                c0 = sum(widths[:t])
                load_tile((W_IN + t) % 2, (W_IN + t) // 2,
                          quarters((W_IN + t) % 2, w_in, slice(c0, c0 + widths[t]), widths[t]))
            w_qb, w_kvb = rows_view(mla_w_qb[0]), rows_view(mla_w_kvb[0])
            with sp.Fori(0, mla.groups) as g:
                for t, (w, n) in enumerate(((w_qb, 2 * MLA_QK), (w_kvb, 2 * (NOPE + VDIM)))):
                    half, number = mla.w(g, t)
                    load_tile(half, number, quarters(half, w, bass.ds(g * n, n), n))

            def four_tiles(n0, w):
                with sp.Fori(0, 2) as i:
                    for t in range(2):
                        half = (n0 + t) % 2
                        load_tile(half, (n0 + t) // 2 + i,
                                  quarters(half, w, bass.ds(i * 2 * TILE + t * TILE, TILE), TILE))

            def after_attention(at, g):
                four_tiles(W_O[at.layer], rows_view((mla_w_o, fox_w_o)[at.layer][0]))
                at.ot_done.done(sp, at.groups - 1, at.ot_done.n - 1)
                load_gains(2 * at.layer + 1, g)
                n0, w = W_PQ[at.layer], rows_view(peer_w_q[at.layer])
                with sp.Fori(0, PHEADS // 2) as i:
                    for t in range(2):
                        half = (n0 + t) % 2
                        load_tile(half, (n0 + t) // 2 + i,
                                  quarters(half, w, bass.ds(i * 4 * P + t * 2 * P, 2 * P), 2 * P))

            after_attention(mla, norm_ffn_g[0:1, :])
            def fox_tile(g, t):
                half, number = fox.w(g, t)
                load_tile(half, number, quarters(half, fw, bass.ds(g * TILE + t * D, TILE), TILE))

            fw = rows_view(fox_w_in[0])
            load_tile(W_F % 2, W_F // 2, quarters(W_F % 2, fw, slice(4 * D, 4 * D + HEADS), HEADS))
            fox_tile(0, 0)
            sp.wait_ge(peer_added, NB)
            load_gains(2, norm_mix_g[1:2, :])
            for t in range(1, 4):
                fox_tile(0, t)
            with sp.Fori(1, fox.groups) as g:
                for t in range(4):
                    fox_tile(g, t)
            after_attention(fox, norm_ffn_g[1:2, :])
            for b in range(NB):
                sp.wait_ge(peer_added, NB + b + 1)
                sp.dma_start(out[0, b * P:(b + 1) * P, :], resid[:, b, :]).then_inc(stored, 16)
            sp.wait_ge(stored, 16 * NB)

        @block.gpsimd
        def _(pool):
            n = [0]

            def made(ins):
                n[0] += 1
                ins.then_inc(consts_made, 1)

            made(pool.memset(ident[:, :], 0.0))
            made(pool.memset(mask_mla[:, :], 0.0))
            made(pool.memset(mask_fox[:, :], 0.0))
            made(pool.memset(upto[:, :], 1.0))
            made(pool.iota(iota[:, :], [[1, TOPK]], base=0, channel_multiplier=0,
                           allow_small_or_imprecise_dtypes=True))
            pool.wait_ge(consts_made, n[0])
            made(pool.affine_select(out=ident[:, :], in_=ident[:, :], compare_op=ALU.not_equal, fill=1.0,
                                    base=0, pattern=[[-1, P]], channel_multiplier=1))
            made(pool.affine_select(out=mask_fox[:, P:T], in_=mask_fox[:, P:T], compare_op=ALU.is_ge,
                                    fill=MASKED, base=0, pattern=[[-1, P]], channel_multiplier=1))
            made(pool.affine_select(out=mask_mla[:, P + CHUNK:T], in_=mask_mla[:, P + CHUNK:T],
                                    compare_op=ALU.is_ge, fill=MASKED, base=-CHUNK,
                                    pattern=[[0, CHUNK]], channel_multiplier=1))
            made(pool.affine_select(out=upto[:, 0:P], in_=upto[:, 0:P], compare_op=ALU.is_ge, fill=0.0,
                                    base=0, pattern=[[1, P]], channel_multiplier=-1))
            assert n[0] == N_CONST

            def unit(layer, number, p):
                pool.wait_ge(index_ready, number + 1)
                for s in range(SLOTS):
                    r = s % RING
                    slot = number * SLOTS + s
                    pool.wait_ge(dot_done, slot + 1)
                    pool.sem_inc(held["pool"], 1)
                    pool.indirect_dma_start(u_ring[:, r, :], None, peer_u.rearrange("l n d -> (l n) d"),
                                            bass.IndirectOffsetOnAxis(index[:, p, s:s + 1], 0)).then_inc(u_full[r], 16)
                    pool.wait_ge(mm_done, slot + 1)
                    pool.sem_inc(held["pool"], 1)
                    pool.indirect_dma_start(v_ring[:, r, :], None, peer_v.rearrange("l n d -> (l n) d"),
                                            bass.IndirectOffsetOnAxis(index[:, p, s:s + 1], 0)).then_inc(v_full[r], 16)

            for layer in range(2):
                with pool.Fori(0, NB * PHEADS // 2) as i:
                    for p in range(2):
                        unit(layer, layer * NB * PHEADS + 2 * i + p, p)

        @block.tensor
        def _(pe):
            for s in (*w_used,):
                pe.sem_inc(s, 1)
            pe.sem_inc(mm_done, RING)
            pe.sem_inc(match_full, 1)

            def transpose(dst, src, k=P):
                return pe.transpose(dst, src, ident[0:k, 0:k])

            def norm_transposes(p):
                for b in range(NB):
                    pe.wait_ge(norm_done, 2 * p + b + 1)
                    for q in range(4):
                        if b:
                            pe.wait_ge(ht_done, 8 * p + q + 1)
                        for c in range(4):
                            k = 4 * q + c
                            last = transpose(psum[:, 4 + q, c * P:(c + 1) * P], normed[:, b, k * P:(k + 1) * P])
                        last.then_inc(ht_full, 1)
                pe.wait_ge(ht_done, 8 * (p + 1))

            def gemm(wt, gt, nk, n, stationary):
                (wh, wn), (gh, gn) = wt, gt
                pe.wait_ge(w_full[wh], 64 * (wn + 1))
                for b in range(NB):
                    pe.wait_ge(evac[gh], 2 * gn + b + 1)
                    for k in range(nk):
                        last = pe.matmul(gbank(gh, b)[:, 0:n], stationary[:, k, b * P:(b + 1) * P],
                                         wbuf[:, wh, k, 0:n], start=k == 0, stop=k == nk - 1)
                    last.then_inc(g_full[gh], 1)
                return wh

            def used(wh):
                pe.sem_inc(w_used[wh], 1)

            def sub_keys():
                pe.wait_ge(small_loaded, 16 * N_SMALL)
                for m in range(4):
                    last = transpose(psum[:, 7, m * P:(m + 1) * P], keys_n[:, m, :])
                last.then_inc(keys_full, 1)

            def latent():
                for t, n in enumerate((Q_RANK, KV_RANK, ROPE)):
                    tile = ((W_IN + t) % 2, (W_IN + t) // 2)
                    gemm_and_free(tile, ((G_IN + t) % 2, (G_IN + t) // 2), KC, n, normedT)
                for t in range(2):
                    for b in range(NB):
                        pe.wait_ge(lat_norm, 2 * t + b + 1)
                        if t:
                            pe.wait_ge(lat_done, b + 1)
                        for c in range(RC):
                            last = transpose(sbank(b)[:, c * P:(c + 1) * P], (qn, kn)[t][:, b, c * P:(c + 1) * P])
                        last.then_inc(lat_full, 1)

            def gemm_and_free(wt, gt, nk, n, stationary):
                gemm(wt, gt, nk, n, stationary)
                (gh, gn) = gt
                pe.wait_ge(g_full[gh], 2 * gn + 2)
                used(wt[0])

            def forget_decay():
                gemm_and_free((W_F % 2, W_F // 2), (G_F % 2, G_F // 2), KC, HEADS, normedT)
                pe.wait_ge(forget_log, 1)
                pe.matmul(psum[0:HEADS, 6, 0:T], fl[:, 4, 0, :], upto[:, :], start=True, stop=False)
                pe.matmul(psum[0:HEADS, 6, P:T], fl[:, 4, 1, :], upto[:, 0:P], start=False,
                          stop=True).then_inc(decay_full, 1)

            def qk_transposes(at, g, kind):
                src = (qn, kn)[kind]
                for b in range(NB):
                    at.qk_norm.done(pe, g, 2 * kind + b)
                    if kind == 0:
                        at.masked.turn_before(pe, g)
                    else:
                        at.t_done.done(pe, g, b)
                    for c in range(4 if at.fox else 3):
                        last = transpose(sbank(b)[:, c * P:(c + 1) * P], src[:, b, c * P:(c + 1) * P])
                    last.then_inc(at.t_full.sem, 1)

            def attention(at, g):
                nj = len(at.jobs)

                def logits(j):
                    h, b = at.jobs[j]
                    r, n = j % 2, (b + 1) * P
                    if j == 0:
                        at.t_done.done(pe, g, 3)
                    at.masked.done(pe, g, j, back=2)
                    dst = sbank(r)[:, 0:n]
                    pe.matmul(dst, qT[:, h, b * P:(b + 1) * P], kT[:, h, 0:n], start=True, stop=False)
                    if at.fox:
                        last = pe.matmul(dst, upto[0:HEADS, P:T], decay_rows[0:HEADS, bass.ds(at.nh * g + h, 1), 0:n].rearrange("p o t -> p (o t)"),
                                         start=False, stop=True)
                    else:
                        k0 = h * ROPE
                        last = pe.matmul(dst, qropeT[k0:k0 + ROPE, b * P:(b + 1) * P],
                                         kropeT[k0:k0 + ROPE, 0:n], start=False, stop=True)
                    last.then_inc(at.s_full.sem, 1)

                def probs_transposes(j):
                    h, b = at.jobs[j]
                    at.exped.done(pe, g, j)
                    at.pt_done.done(pe, g, j, back=2)
                    for k in range(b + 1):
                        last = transpose(pt_bank(j % 2)[:, k, :], probs[:, j % 2, k * P:(k + 1) * P])
                    last.then_inc(at.pt_full.sem, 1)

                def values(j):
                    h, b = at.jobs[j]
                    at.pt_done.done(pe, g, j)
                    at.og_done.done(pe, g, j, back=2)
                    if j == 0:
                        for t in range(at.tiles - 2, at.tiles):
                            gh, gn = at.g(g, t)
                            pe.wait_ge(evac[gh], 2 * gn + 4)
                    for k in range(b + 1):
                        v = raw_v[:, k, h * P:(h + 1) * P] if at.fox else raw_k[:, k, (2 * h + 1) * P:(2 * h + 2) * P]
                        last = pe.matmul(o_bank(j % 2), probsT[:, j % 2, k, :], v, start=k == 0, stop=k == b)
                    last.then_inc(at.o_full.sem, 1)

                def out_transposes(j):
                    at.og_done.done(pe, g, j)
                    at.ot_done.done(pe, g, j, back=2)
                    transpose(ot_bank(j % 2), og[:, j % 2, :]).then_inc(at.ot_full.sem, 1)

                for step in range(nj + 3):
                    for lag, stage in enumerate((logits, probs_transposes, values, out_transposes)):
                        if 0 <= step - lag < nj:
                            stage(step - lag)

            def free_banks(at, g):
                at.og_done.turn_before(pe, g)
                at.ot_done.turn_before(pe, g)

            def mla_groups():
                for e in (mla.t_full, mla.s_full, mla.pt_full, mla.o_full, mla.ot_full):
                    e.credit(pe)
                pe.wait_ge(lat_done, 4)
                with pe.Fori(0, mla.groups) as g:
                    free_banks(mla, g)
                    gemm_and_free(mla.w(g, 0), mla.g(g, 0), RC, 2 * MLA_QK, cqT)
                    gemm_and_free(mla.w(g, 1), mla.g(g, 1), RC, 2 * (NOPE + VDIM), ckvT)
                    qk_transposes(mla, g, 0)
                    qk_transposes(mla, g, 1)
                    attention(mla, g)

            def fox_groups():
                for e in (fox.t_full, fox.s_full, fox.pt_full, fox.o_full, fox.ot_full):
                    e.credit(pe)
                with pe.Fori(0, fox.groups) as g:
                    free_banks(fox, g)
                    for t in range(4):
                        gemm_and_free(fox.w(g, t), fox.g(g, t), KC, TILE, normedT)
                        if t in (1, 2):
                            qk_transposes(fox, g, t - 1)
                    pe.wait_ge(decay_ready, 2)
                    attention(fox, g)

            def out_projection(at):
                at.ot_done.done(pe, at.groups - 1, at.ot_done.n - 1)
                w0, g0 = W_O[at.layer], G_O[at.layer]
                with pe.Fori(0, 2) as i:
                    for t in range(2):
                        gemm_and_free(((w0 + t) % 2, (w0 + t) // 2 + i), ((g0 + t) % 2, (g0 + t) // 2 + i),
                                      KC, TILE, attnT)

            def queries(layer, h, c, ks):
                wh = (W_PQ[layer] + h[1]) % 2
                head = PHEADS * layer + h[0] + h[1]
                if ks[0] == 0:
                    pe.wait_ge(w_full[wh], 64 * ((W_PQ[layer] + h[1]) // 2 + h[2] + 1))
                    pe.wait_ge(query_done, 2 * head + c + 1)
                for k in ks:
                    last = pe.matmul(psum[:, 4 + c, 0:T], wbuf[:, wh, k, c * P:(c + 1) * P],
                                     normedT[:, k, :], start=k == 0, stop=k == KC - 1)
                if ks[-1] == KC - 1:
                    last.then_inc(query_full, 1)

            def match(layer, h):
                wh = (W_PQ[layer] + h[1]) % 2
                head = PHEADS * layer + h[0] + h[1]
                pe.wait_ge(query_full, 2 * head + 2)
                used(wh)
                pe.wait_ge(query_done, 2 * head + 4)
                pe.wait_ge(match_done, head + 1)
                for b in range(NB):
                    for c in range(2):
                        last = pe.matmul(psum[:, 6 + b, c * KEYS:(c + 1) * KEYS], peer_qT[:, c, b * P:(b + 1) * P],
                                         keysT[:, 2 * layer + c, :], start=True, stop=True)
                last.then_inc(match_full, 1)

            def peer(layer):
                first = (0, 0, 0)
                for c in range(2):
                    queries(layer, first, c, range(KC))
                match(layer, first)

                def pair_of_units(i, b, last):
                    for p in range(2):
                        number = (NB * layer + b) * PHEADS + 2 * i + p
                        ahead = b == 0 and not (last and p)
                        head = (2 * i, p + 1, i)
                        for s in range(SLOTS):
                            r = s % RING
                            slot = number * SLOTS + s
                            pe.wait_ge(diag_ready, slot + 1 + RING)
                            pe.wait_ge(v_full[r], 16 * (number * (SLOTS // RING) + s // RING + 1))
                            for q in range(4):
                                mm = pe.matmul(psum[:, 4 * b + q, :], diag[:, r, :],
                                               v_ring[:, r, q * TILE:(q + 1) * TILE],
                                               start=False, stop=False, skip_group_check=True)
                            mm.then_inc(mm_done, 1)
                            if ahead and s < MATCH_AT:
                                queries(layer, head, s // 4, range(s % 4 * 4, s % 4 * 4 + 4))
                            if ahead and s == MATCH_AT:
                                match(layer, head)

                for b in range(NB):
                    pe.wait_ge(acc_zero, 2 * layer + b + 1)
                    with pe.Fori(0, PHEADS // 2 - 1) as i:
                        pair_of_units(i, b, False)
                    pair_of_units(PHEADS // 2 - 1, b, True)

            pe.wait_ge(consts_made, N_CONST)
            norm_transposes(0)
            sub_keys()
            latent()
            mla_groups()
            out_projection(mla)
            norm_transposes(1)
            peer(0)
            norm_transposes(2)
            forget_decay()
            fox_groups()
            out_projection(fox)
            norm_transposes(3)
            peer(1)

        @block.scalar
        def _(act):
            chain = Chain(act, act_steps)
            for s in evac:
                act.sem_inc(s, 2)
            act.sem_inc(query_done, 2)
            act.sem_inc(match_done, 1)
            act.sem_inc(diag_ready, RING)
            count = 0
            for dst, src in (
                (pos_i[:, 0:1], positions[0:1, 0:P].rearrange("o p -> p o")),
                (pos_i[:, 1:2], positions[0:1, P:T].rearrange("o p -> p o")),
                (inv_row[:, :], inv_freq.broadcast_to([P, HALF])),
                (g_cols[:, 0:1], mla_g_q[0:1, 0:NOPE].rearrange("o p -> p o")),
                (g_cols[:, 1:2], mla_g_k[0:1, 0:NOPE].rearrange("o p -> p o")),
                (g_cols[:, 2:3], fox_g_q.rearrange("o p -> p o")),
                (g_cols[:, 3:4], fox_g_k.rearrange("o p -> p o")),
                (g_qrope[:, :], mla_g_q[0:1, NOPE:MLA_QK].broadcast_to([P, ROPE])),
                (g_krope[:, :], mla_g_k[0:1, NOPE:MLA_QK].broadcast_to([P, ROPE])),
                (g_qa[:, :], mla_g_qa.broadcast_to([P, Q_RANK])),
                (g_kva[:, :], mla_g_kva.broadcast_to([P, KV_RANK])),
                (b_f[:, :], fox_b_f.broadcast_to([P, HEADS])),
                (keys_n[:, :, :], peer_sub_keys.rearrange("l c n d -> n (l c) d")),
            ):
                act.dma_start(dst, src).then_inc(small_loaded, 16)
                count += 1
            assert count == N_SMALL

            def square_root(dst, src, width, ready):
                return nc.scalar.activation(dst, src, ACT.Sqrt, bias=EPS, scale=1.0 / width).then_inc(ready, 1)

            def norm(p):
                for b in range(NB):
                    if p == 0:
                        act.wait_ge(x_loaded, 16 * NB)
                    elif p % 2:
                        act.wait_ge(o_added, p // 2 + 1)
                    else:
                        act.wait_ge(peer_added, NB)
                    chain.step(nc.scalar.activation(squares[:, b, :], resid[:, b, :], ACT.Square,
                                                    accum_out=n_sum[:, b:b + 1]))
                    chain.settle()
                    square_root(n_root[:, b:b + 1], n_sum[:, b:b + 1], D, norm_root)
                for b in range(NB):
                    for q in range(4):
                        act.wait_ge(ht_full, 8 * p + 4 * b + q + 1)
                        nc.scalar.activation(
                            normedT[:, 4 * q:4 * q + 4, b * P:(b + 1) * P],
                            psum[:, 4 + q, :].rearrange("p (k t) -> p k t", k=4), ACT.Copy).then_inc(ht_done, 1)

            def copy_out(gt, b, dst, n, func=ACT.Copy):
                gh, gn = gt
                act.wait_ge(g_full[gh], 2 * gn + b + 1)
                nc.scalar.activation(dst, gbank(gh, b)[:, 0:n], func).then_inc(evac[gh], 1)

            def latent():
                for t, (dst, n) in enumerate(((raw_q, Q_RANK), (raw_k, KV_RANK), (raw_v, ROPE))):
                    for b in range(NB):
                        copy_out(((G_IN + t) % 2, (G_IN + t) // 2), b, dst[:, b, 0:n], n)
                for t in range(2):
                    act.wait_ge(lat_ss, t + 1)
                    square_root(l_root[:, 2 * t:2 * t + 2], l_sum[:, 2 * t:2 * t + 2], Q_RANK, lat_root)
                for t in range(2):
                    for b in range(NB):
                        act.wait_ge(lat_full, 2 * t + b + 1)
                        nc.scalar.activation((cqT, ckvT)[t][:, :, b * P:(b + 1) * P],
                                             sbank(b)[:, 0:RC * P].rearrange("p (c t) -> p c t", c=RC),
                                             ACT.Copy).then_inc(lat_done, 1)

            def forget():
                act.wait_ge(forget_in, 1)
                chain.step(nc.scalar.activation(fl[:, 3], fl[:, 1], ACT.Exp, scale=-1.0))
                chain.settle()
                nc.scalar.activation(fl[:, 3], fl[:, 3], ACT.Ln, bias=1.0).then_inc(forget_ln, 1)

            def roots(at, g, kind):
                at.ss_ready.done(act, g, kind)
                root, total = ((h_root, h_sum), (k_root, k_sum))[kind] if not at.fox else (h_root, h_sum)
                n = NB * at.nh
                square_root(root[:, 0:n], total[:, 0:n], HD if at.fox else MLA_QK, at.root_ready.sem)

            def transposed(at, g, kind):
                dst = (qT, kT)[kind]
                gain = g_cols[:, 2 * at.fox + kind:2 * at.fox + kind + 1]
                if kind == 0:
                    at.s_full.turn_before(act, g)
                for b in range(NB):
                    at.t_full.done(act, g, 2 * kind + b)
                    n = at.nh
                    last = nc.scalar.activation(dst[:, 0:n, b * P:(b + 1) * P],
                                                sbank(b)[:, 0:n * P].rearrange("p (h t) -> p h t", h=n),
                                                ACT.Copy, scale=gain)
                    if not at.fox:
                        last = nc.scalar.activation((qropeT, kropeT)[kind][:, b * P:(b + 1) * P],
                                                    sbank(b)[:, n * P:(n + 1) * P], ACT.Copy)
                    last.then_inc(at.t_done.sem, 1)

            def attention(at, g):
                nj = len(at.jobs)

                def exponentials(j):
                    h, b = at.jobs[j]
                    n = (b + 1) * P
                    at.negated.done(act, g, j)
                    at.pt_full.done(act, g, j, back=2)
                    nc.scalar.activation(probs[:, j % 2, 0:n], masked[:, j % 2, 0:n], ACT.Exp,
                                         bias=neg_max[:, j:j + 1],
                                         accum_out=row_sum[:, j:j + 1]).then_inc(at.exped.sem, 1)

                def probs_copy(j):
                    h, b = at.jobs[j]
                    at.pt_full.done(act, g, j)
                    at.o_full.done(act, g, j, back=2)
                    nc.scalar.activation(probsT[:, j % 2, 0:b + 1, :], pt_bank(j % 2)[:, 0:b + 1, :],
                                         ACT.Copy).then_inc(at.pt_done.sem, 1)

                def out_copy(j):
                    h, b = at.jobs[j]
                    at.ot_full.done(act, g, j)
                    act.sem_inc(held["act"], 1)
                    nc.scalar.activation(attnT[:, bass.ds(at.nh * g + h, 1), b * P:(b + 1) * P], ot_bank(j % 2).unsqueeze(1),
                                         ACT.Copy).then_inc(at.ot_done.sem, 1)

                for step in range(nj + 3):
                    if step < nj:
                        exponentials(step)
                    if 0 <= step - 1 < nj:
                        probs_copy(step - 1)
                    if 0 <= step - 3 < nj:
                        out_copy(step - 3)

            def mla_groups():
                for e in (mla.root_ready, mla.t_done, mla.exped, mla.pt_done, mla.ot_done):
                    e.credit(act)
                with act.Fori(0, mla.groups) as g:
                    for b in range(NB):
                        mla.qk_norm.turn_before(act, g, b)
                        copy_out(mla.g(g, 0), b, raw_q[:, b, 0:2 * MLA_QK], 2 * MLA_QK)
                    mla.qk_norm.turn_before(act, g)
                    mla.o_full.turn_before(act, g)
                    for b in range(NB):
                        copy_out(mla.g(g, 1), b, raw_k[:, b, :], TILE)
                    for kind in range(2):
                        roots(mla, g, kind)
                    for kind in range(2):
                        transposed(mla, g, kind)
                    attention(mla, g)

            def fox_groups():
                for e in (fox.root_ready, fox.t_done, fox.exped, fox.pt_done, fox.ot_done):
                    e.credit(act)
                with act.Fori(0, fox.groups) as g:
                    for kind in range(2):
                        for b in range(NB):
                            fox.qk_norm.turn_before(act, g, 2 * kind + b)
                            copy_out(fox.g(g, kind), b, (raw_q, raw_k)[kind][:, b, :], TILE)
                        roots(fox, g, kind)
                        if kind:
                            transposed(fox, g, 0)
                    fox.o_full.turn_before(act, g)
                    for b in range(NB):
                        copy_out(fox.g(g, 2), b, raw_v[:, b, :], TILE)
                    transposed(fox, g, 1)
                    fox.og_done.turn_before(act, g)
                    for b in range(NB):
                        copy_out(fox.g(g, 3), b, gate[:, b, :], TILE, ACT.Sigmoid)
                    attention(fox, g)

            def peer(layer):
                first = NB * PHEADS * layer

                def copy_queries(head, c):
                    act.wait_ge(query_full, 2 * head + c + 1)
                    act.wait_ge(match_full, head + 1)
                    nc.scalar.activation(peer_qT[:, c, :], psum[:, 4 + c, 0:T], ACT.Copy).then_inc(query_done, 1)

                def copy_matches(head, number, h):
                    act.wait_ge(match_full, head + 2)
                    act.wait_ge(pick_used, number + 1)
                    nc.scalar.activation(pick_flat, psum[:, 6, 0:2 * KEYS], ACT.Copy).then_inc(pick_ready, 1)
                    nc.scalar.activation(scores[:, bass.ds(h * 2 * KEYS, 2 * KEYS)] if not isinstance(h, int) else
                                         scores[:, h * 2 * KEYS:(h + 1) * 2 * KEYS],
                                         psum[:, 7, 0:2 * KEYS], ACT.Copy).then_inc(match_done, 1)

                def fetch(number, h):
                    act.wait_ge(pick_used, number + 1)
                    act.sem_inc(held["act"], 1)
                    nc.scalar.activation(pick_flat, scores[:, bass.ds(h * 2 * KEYS, 2 * KEYS)],
                                         ACT.Copy).then_inc(pick_ready, 1)

                def soften(number):
                    act.wait_ge(best_ready, number + 1)
                    nc.scalar.activation(soft_e[:, :], best[:, :], ACT.Exp, bias=soft[:, 0:1],
                                         accum_out=soft[:, 1:2]).then_inc(exp_ready, 1)

                def slots(number, p, which):
                    for s in which:
                        r = s % RING
                        slot = number * SLOTS + s
                        act.wait_ge(dot_done, slot + 1 + RING)
                        chain.step(nc.scalar.activation(acts[:, 0, r:r + 1], dots[:, r:r + 1], ACT.Gelu))
                        chain.settle()
                        if s == 0:
                            act.wait_ge(gate_ready, number + 1)
                        chain.step(nc.scalar.activation(acts[:, 1, r:r + 1], acts[:, 0, r:r + 1], ACT.Copy,
                                                        scale=gates[:, p, s:s + 1]))
                        act.wait_ge(mm_done, slot + 1)
                        chain.settle()
                        nc.scalar.activation(diag[:, r, :], ident[:, :], ACT.Copy,
                                             scale=acts[:, 1, r:r + 1]).then_inc(diag_ready, 1)

                head = PHEADS * layer
                for c in range(2):
                    copy_queries(head, c)
                copy_matches(head, first, 0)
                soften(first)

                def pair_of_units(i, b, last):
                    for p in range(2):
                        h = 2 * i + p
                        number = first + b * PHEADS + h
                        ahead = b == 0 and not (last and p)
                        if ahead:
                            slots(number, p, range(0, 5))
                            copy_queries(head + h + 1, 0)
                            slots(number, p, range(5, MATCH_AT + 1))
                            copy_queries(head + h + 1, 1)
                            slots(number, p, range(MATCH_AT + 1, MATCH_AT + 2))
                            copy_matches(head + h + 1, number + 1, h + 1)
                        else:
                            slots(number, p, range(0, MATCH_AT + 2))
                            if b == 0:
                                fetch(number + 1, 0)
                            elif not (last and p):
                                fetch(number + 1, h + 1)
                        slots(number, p, range(MATCH_AT + 2, CHOOSE_AT))
                        if not (last and p and b == NB - 1):
                            soften(number + 1)
                        slots(number, p, range(CHOOSE_AT, SLOTS))

                looped = PHEADS // 2 - 1
                for b in range(NB):
                    with act.Fori(0, looped) as i:
                        chain.enter(i, 2 * 2 * SLOTS)
                        pair_of_units(i, b, False)
                    chain.leave(looped)
                    pair_of_units(looped, b, True)

            norm(0)
            act.wait_ge(keys_full, 1)
            nc.scalar.activation(keysT[:, :, :], psum[:, 7, :].rearrange("p (m n) -> p m n", m=4),
                                 ACT.Copy).then_inc(keys_done, 1)
            act.wait_ge(angles_ready, 1)
            for m in range(2):
                last = nc.scalar.activation(ang[:, 2 + m], ang[:, m], ACT.Sin)
            last.then_inc(trig_ready, 1)
            latent()
            mla_groups()
            norm(1)
            peer(0)
            norm(2)
            forget()
            fox_groups()
            norm(3)
            peer(1)

        @block.vector
        def _(dve):
            V = nc.vector
            chain = Chain(dve, dve_steps)

            def step(ins):
                chain.step(ins)

            def hold():
                dve.sem_inc(held["dve"], 1)

            dve.sem_inc(dot_done, RING)
            dve.sem_inc(pick_used, 1)

            def angles():
                dve.wait_ge(small_loaded, 16 * N_SMALL)
                dve.wait_ge(consts_made, N_CONST)
                step(V.tensor_copy(pos_f[:, :], pos_i[:, :]))
                chain.settle()
                for b in range(NB):
                    step(V.tensor_scalar(ang[:, 0, b, :], inv_row[:, :], pos_f[:, b:b + 1], None, ALU.mult))
                chain.settle()
                step(V.tensor_scalar(ang[:, 1], ang[:, 0], 1.0 / TWO_PI, ROUND_MAGIC, ALU.mult, ALU.add))
                chain.settle()
                step(V.tensor_scalar(ang[:, 1], ang[:, 1], ROUND_MAGIC, None, ALU.subtract))
                for part in (PI_A, PI_B, PI_C):
                    chain.settle()
                    step(V.scalar_tensor_tensor(out=ang[:, 0], in0=ang[:, 1], scalar=-part, in1=ang[:, 0],
                                                op0=ALU.mult, op1=ALU.add))
                chain.settle()
                step(V.tensor_scalar(ang[:, 0], ang[:, 0], PI_SAFE, -PI_SAFE, ALU.min, ALU.max))
                chain.settle()
                step(V.scalar_tensor_tensor(out=ang[:, 1], in0=ang[:, 0], scalar=-1.0, in1=ang[:, 0],
                                            op0=ALU.mult, op1=ALU.max))
                chain.settle()
                V.tensor_scalar(ang[:, 1], ang[:, 1], -1.0, TWO_PI / 4, ALU.mult, ALU.add).then_inc(angles_ready, 1)
                step(V.tensor_scalar(g_cols[:, 0:1], g_cols[:, 0:1], MLA_QK ** -0.5, None, ALU.mult))
                step(V.tensor_scalar(g_cols[:, 2:3], g_cols[:, 2:3], HD ** -0.5, None, ALU.mult))
                step(V.tensor_scalar(g_qrope[:, :], g_qrope[:, :], MLA_QK ** -0.5, None, ALU.mult))
                dve.wait_ge(trig_ready, 1)
                step(V.tensor_scalar(sin2[:, :, 0:HALF], ang[:, 2], -1.0, None, ALU.mult))
                step(V.tensor_copy(sin2[:, :, HALF:ROPE], ang[:, 2]))
                step(V.tensor_copy(cos2[:, :, 0:HALF], ang[:, 3]))
                step(V.tensor_copy(cos2[:, :, HALF:ROPE], ang[:, 3]))
                chain.settle()

            def norm(p):
                for b in range(NB):
                    dve.wait_ge(norm_root, 2 * p + b + 1)
                    step(V.reciprocal(n_inv[:, b:b + 1], n_root[:, b:b + 1]))
                    chain.settle()
                    dve.wait_ge(gains_loaded, 16 * (p + 1))
                    V.scalar_tensor_tensor(out=normed[:, b, :], in0=resid[:, b, :], scalar=n_inv[:, b:b + 1],
                                           in1=gain_row, op0=ALU.mult, op1=ALU.mult).then_inc(norm_done, 1)

            def sum_squares(src, junk, dst):
                return V.tensor_tensor_reduce(junk, src, src, 1.0, 0.0, ALU.mult, ALU.add, dst)

            def rotate(dst, src, b, heads, ta, tb):
                def over_heads(a):
                    return a.unsqueeze(1).broadcast_to([P, heads, a.shape[-1]])
                step(V.tensor_tensor(ta, src, over_heads(cos2[:, b, :]), ALU.mult))
                step(V.tensor_tensor(tb[:, :, 0:HALF], src[:, :, HALF:ROPE], over_heads(sin2[:, b, 0:HALF]), ALU.mult))
                step(V.tensor_tensor(tb[:, :, HALF:ROPE], src[:, :, 0:HALF], over_heads(sin2[:, b, HALF:ROPE]), ALU.mult))
                chain.settle()
                return V.tensor_tensor(dst, ta, tb, ALU.add)

            def latent():
                for t, raw in enumerate((raw_q, raw_k)):
                    for b in range(NB):
                        dve.wait_ge(evac[(G_IN + t) % 2], 2 * ((G_IN + t) // 2) + b + 3)
                        last = sum_squares(raw[:, b, :], (qn, kn)[t][:, b, :], l_sum[:, 2 * t + b:2 * t + b + 1])
                    last.then_inc(lat_ss, 1)
                for t, (raw, g) in enumerate(((raw_q, g_qa), (raw_k, g_kva))):
                    dve.wait_ge(lat_root, t + 1)
                    step(V.reciprocal(l_inv[:, 2 * t:2 * t + 2], l_root[:, 2 * t:2 * t + 2]))
                    chain.settle()
                    for b in range(NB):
                        V.scalar_tensor_tensor(out=(qn, kn)[t][:, b, :], in0=raw[:, b, :],
                                               scalar=l_inv[:, 2 * t + b:2 * t + b + 1], in1=g[:, :],
                                               op0=ALU.mult, op1=ALU.mult).then_inc(lat_norm, 1)
                for b in range(NB):
                    dve.wait_ge(evac[(G_IN + 2) % 2], 2 * ((G_IN + 2) // 2) + b + 3)
                    kr = raw_v[:, b, 0:ROPE]
                    step(sum_squares(kr, tmp_a[:, b, 1, :], rope_sum[:, b:b + 1]))
                    chain.settle()
                    step(V.tensor_tensor(raw_v[:, b, ROPE:2 * ROPE], kr, g_krope[:, :], ALU.mult))
                    chain.settle()
                    step(rotate(k_rot[:, b:b + 1, :], raw_v[:, b:b + 1, ROPE:2 * ROPE], b, 1,
                                tmp_a[:, b, 0:1, :], tmp_b[:, b, 0:1, :]))
                chain.settle()

            def forget():
                gh, gn = G_F % 2, G_F // 2
                for b in range(NB):
                    dve.wait_ge(g_full[gh], 2 * gn + b + 1)
                    V.tensor_tensor(fl[:, 0, b, :], gbank(gh, b)[:, 0:HEADS], b_f[:, :], ALU.add).then_inc(evac[gh], 1)
                dve.wait_ge(evac[gh], 2 * gn + 4)
                step(V.tensor_scalar(fl[:, 2], fl[:, 0], 0.0, None, ALU.min))
                V.scalar_tensor_tensor(out=fl[:, 1], in0=fl[:, 0], scalar=-1.0, in1=fl[:, 0],
                                       op0=ALU.mult, op1=ALU.max).then_inc(forget_in, 1)
                dve.wait_ge(forget_ln, 1)
                chain.settle()
                V.tensor_tensor(fl[:, 4], fl[:, 2], fl[:, 3], ALU.subtract).then_inc(forget_log, 1)
                dve.wait_ge(decay_full, 1)
                V.tensor_copy(decayT[0:HEADS, :], psum[0:HEADS, 6, 0:T]).then_inc(decay_ready, 1)
                dve.wait_ge(decay_ready, 1)
                V.scalar_tensor_tensor(out=decay_rows[0:HEADS, :, :],
                                       in0=decayT[0:HEADS, :].unsqueeze(1).broadcast_to([HEADS, HEADS, T]),
                                       scalar=-1.0,
                                       in1=ident[0:HEADS, 0:HEADS].unsqueeze(2).broadcast_to([HEADS, HEADS, T]),
                                       op0=ALU.mult, op1=ALU.mult).then_inc(decay_ready, 1)

            def head_norms(at, g, kind):
                raw, dst = ((raw_q, qn), (raw_k, kn))[kind]
                total, root, inv = ((h_sum, h_root, h_inv), (k_sum, k_root, k_inv))[kind] if not at.fox else (
                    h_sum, h_root, h_inv)
                nh = at.nh
                gh, gn = at.g(g, kind)
                for b in range(NB):
                    dve.wait_ge(evac[gh], 2 * gn + b + 3)
                    at.t_full.turn_before(dve, g, 2 * kind + b)
                    for h in range(nh):
                        if at.fox:
                            src = raw[:, b, h * P:(h + 1) * P]
                        elif kind == 0:
                            src = raw[:, b, h * MLA_QK:(h + 1) * MLA_QK]
                        else:
                            src = raw[:, b, 2 * h * P:(2 * h + 1) * P]
                        last = sum_squares(src, dst[:, b, h * src.shape[-1]:(h + 1) * src.shape[-1]], total[:, b * nh + h:b * nh + h + 1])
                        if not at.fox and kind:
                            step(last)
                if not at.fox and kind:
                    chain.settle()
                    last = V.tensor_tensor(total[:, 0:2 * nh].rearrange("p (b h) -> p b h", b=NB),
                                           total[:, 0:2 * nh].rearrange("p (b h) -> p b h", b=NB),
                                           rope_sum.unsqueeze(2).broadcast_to([P, NB, nh]), ALU.add)
                last.then_inc(at.ss_ready.sem, 1)
                at.root_ready.done(dve, g, kind)
                step(V.reciprocal(inv[:, 0:2 * nh], root[:, 0:2 * nh]))
                chain.settle()
                for b in range(NB):
                    def per_head(n):
                        return inv[:, b * nh:(b + 1) * nh].unsqueeze(2).broadcast_to([P, nh, n])
                    if at.fox:
                        V.tensor_tensor(dst[:, b, :].rearrange("p (h d) -> p h d", h=nh),
                                        raw[:, b, :].rearrange("p (h d) -> p h d", h=nh), per_head(P),
                                        ALU.mult).then_inc(at.qk_norm.sem, 1)
                        continue
                    nope = dst[:, b, 0:nh * P].rearrange("p (h d) -> p h d", h=nh)
                    rope = dst[:, b, nh * P:nh * P + nh * ROPE].rearrange("p (h d) -> p h d", h=nh)
                    if kind == 0:
                        src = raw[:, b, 0:nh * MLA_QK].rearrange("p (h d) -> p h d", h=nh)
                        step(V.tensor_tensor(nope, src[:, :, 0:NOPE], per_head(NOPE), ALU.mult))
                        step(V.tensor_tensor(rope, src[:, :, NOPE:MLA_QK], per_head(ROPE), ALU.mult))
                        chain.settle()
                        step(V.tensor_tensor(rope, rope, g_qrope[:, :].unsqueeze(1).broadcast_to([P, nh, ROPE]), ALU.mult))
                        chain.settle()
                        rotate(rope, rope, b, nh, tmp_a[:, b], tmp_b[:, b]).then_inc(at.qk_norm.sem, 1)
                    else:
                        src = raw[:, b, :].rearrange("p (h d) -> p h d", h=nh)
                        step(V.tensor_tensor(nope, src[:, :, 0:NOPE], per_head(NOPE), ALU.mult))
                        V.tensor_tensor(rope, k_rot[:, b, :].unsqueeze(1).broadcast_to([P, nh, ROPE]),
                                        per_head(ROPE), ALU.mult).then_inc(at.qk_norm.sem, 1)

            def attention(at, g):
                nj = len(at.jobs)
                mask = mask_fox if at.fox else mask_mla

                def mask_and_max(j):
                    h, b = at.jobs[j]
                    n = (b + 1) * P
                    at.s_full.done(dve, g, j)
                    at.exped.done(dve, g, j, back=2)
                    hold()
                    V.tensor_tensor_reduce(masked[:, j % 2, 0:n], sbank(j % 2)[:, 0:n], mask[:, T - n:T], 1.0,
                                           LOWEST, ALU.add, ALU.max, row_max[:, j:j + 1]).then_inc(at.masked.sem, 1)
                    at.masked.done(dve, g, j)
                    V.tensor_scalar(neg_max[:, j:j + 1], row_max[:, j:j + 1], -1.0, None,
                                    ALU.mult).then_inc(at.negated.sem, 1)

                def finish(j):
                    h, b = at.jobs[j]
                    at.exped.done(dve, g, j)
                    step(V.reciprocal(inv_sum[:, j:j + 1], row_sum[:, j:j + 1]))
                    at.o_full.done(dve, g, j)
                    at.ot_full.done(dve, g, j, back=2)
                    chain.settle()
                    if at.fox:
                        if j == 0:
                            gh, gn = at.g(g, 3)
                            dve.wait_ge(evac[gh], 2 * gn + 4)
                        last = V.scalar_tensor_tensor(out=og[:, j % 2, :], in0=o_bank(j % 2),
                                                      scalar=inv_sum[:, j:j + 1], in1=gate[:, b, h * P:(h + 1) * P],
                                                      op0=ALU.mult, op1=ALU.mult)
                    else:
                        last = V.tensor_scalar(og[:, j % 2, :], o_bank(j % 2), inv_sum[:, j:j + 1], None, ALU.mult)
                    last.then_inc(at.og_done.sem, 1)

                for s in range(nj + 2):
                    if s < nj:
                        mask_and_max(s)
                    if s >= 2:
                        finish(s - 2)

            def groups(at):
                for e in (at.ss_ready, at.qk_norm, at.masked, at.negated, at.og_done):
                    e.credit(dve)
                nj = len(at.jobs)
                per = 2 + nj if at.fox else 2 + nj + 4 + NB * (3 + 3) + NB
                with dve.Fori(0, at.groups) as g:
                    chain.enter(g, per)
                    for kind in range(2):
                        head_norms(at, g, kind)
                    attention(at, g)
                chain.leave(at.groups)

            def add_projection(at):
                g0 = G_O[at.layer]
                with dve.Fori(0, 2) as i:
                    for t in range(2):
                        gh, gn = (g0 + t) % 2, (g0 + t) // 2 + i
                        for b in range(NB):
                            dve.wait_ge(g_full[gh], 2 * gn + b + 1)
                            cols = resid[:, b, bass.ds(i * 2 * TILE + t * TILE, TILE)]
                            V.tensor_tensor(cols, gbank(gh, b), cols, ALU.add).then_inc(evac[gh], 1)
                for t in range(2):
                    dve.wait_ge(evac[(g0 + t) % 2], 2 * ((g0 + t) // 2 + 1) + 4)
                dve.sem_inc(o_added, 1)

            def choose(layer, number, p):
                dve.wait_ge(pick_ready, number + 1)
                hold()
                for c in range(2):
                    step(V.max(top_s[:, c, 0:8], pick[:, c, :]))
                chain.settle()
                hold()
                for c in range(2):
                    step(V.max_index(top_i[:, c, 0:8], top_s[:, c, 0:8], pick[:, c, :]))
                    last = V.match_replace(pick2[:, c, :], top_s[:, c, 0:8], pick[:, c, :], LOWEST)
                    if c:
                        last.then_inc(pick_used, 1)
                    else:
                        step(last)
                chain.settle()
                dve.wait_ge(pick_used, number + 2)
                hold()
                for c in range(2):
                    step(V.max(top_s[:, c, 8:16], pick2[:, c, :]))
                chain.settle()
                hold()
                for c in range(2):
                    step(V.max_index(top_i[:, c, 8:16], top_s[:, c, 8:16], pick2[:, c, :]))
                step(V.tensor_tensor(cand[:, :].rearrange("p (i j) -> p i j", i=TOPK),
                                     top_s[:, 0, :].unsqueeze(2).broadcast_to([P, TOPK, TOPK]),
                                     top_s[:, 1, :].unsqueeze(1).broadcast_to([P, TOPK, TOPK]), ALU.add))
                chain.settle()
                step(V.tensor_scalar(top_if[:, 0, :], top_i[:, 0, :], float(KEYS), None, ALU.mult))
                step(V.tensor_scalar(top_if[:, 1, :], top_i[:, 1, :], float(layer * KEYS * KEYS), None, ALU.add))
                step(V.max(best[:, 0:8], cand[:, :]))
                chain.settle()
                hold()
                step(V.max_index(best_pos[:, 0:8], best[:, 0:8], cand[:, :]))
                step(V.match_replace(cand2[:, :], best[:, 0:8], cand[:, :], LOWEST))
                chain.settle()
                hold()
                step(V.max(best[:, 8:16], cand2[:, :]))
                chain.settle()
                V.tensor_scalar(soft[:, 0:1], best[:, 0:1], -1.0, None, ALU.mult).then_inc(best_ready, 1)
                step(V.max_index(best_pos[:, 8:16], best[:, 8:16], cand2[:, :]))
                chain.settle()
                step(V.tensor_scalar(pair[:, 0, :], best_pos[:, :], 4, None, ALU.logical_shift_right))
                step(V.tensor_scalar(pair[:, 1, :], best_pos[:, :], TOPK - 1, None, ALU.bitwise_and))
                chain.settle()
                step(V.tensor_copy(pair_f[:, :], pair[:, :, :].rearrange("p c k -> p (c k)")))
                chain.settle()
                step(V.tensor_tensor(onehot[:, :, :], pair_f[:, :].unsqueeze(2).broadcast_to([P, 2 * TOPK, TOPK]),
                                     iota[:, :].unsqueeze(1).broadcast_to([P, 2 * TOPK, TOPK]), ALU.is_equal))
                chain.settle()
                hot = onehot[:, :, :].rearrange("p (c k) n -> p c k n", c=2)
                step(V.tensor_tensor(hot, hot, top_if[:, :, :].unsqueeze(2).broadcast_to([P, 2, TOPK, TOPK]), ALU.mult))
                chain.settle()
                step(V.tensor_reduce(key_f[:, :], onehot[:, :, :], AX_X, ALU.add))
                chain.settle()
                if not isinstance(number, int) or number > 0:
                    dve.wait_ge(mm_done, (number - 1) * SLOTS + RING)
                V.tensor_tensor(index[:, p, :], key_f[:, 0:TOPK], key_f[:, TOPK:2 * TOPK],
                                ALU.add).then_inc(index_ready, 1)
                dve.wait_ge(exp_ready, number + 1)
                step(V.reciprocal(soft[:, 2:3], soft[:, 1:2]))
                chain.settle()
                V.tensor_scalar(gates[:, p, :], soft_e[:, :], soft[:, 2:3], None, ALU.mult).then_inc(gate_ready, 1)

            def slots(number, b, which):
                for s in which:
                    r = s % RING
                    slot = number * SLOTS + s
                    dve.wait_ge(u_full[r], 16 * (number * (SLOTS // RING) + s // RING + 1))
                    dve.wait_ge(diag_ready, slot + 1)
                    V.tensor_tensor_reduce(u_ring[:, r, :], u_ring[:, r, :], normed[:, b, :], 1.0, 0.0,
                                           ALU.mult, ALU.add, dots[:, r:r + 1]).then_inc(dot_done, 1)

            def zero_accumulators(b):
                V.memset(psum[:, 4 * b:4 * b + 4, :], 0.0).then_inc(acc_zero, 1)

            def peer(layer):
                first = NB * PHEADS * layer
                zero_accumulators(0)
                choose(layer, first, 0)
                looped = PHEADS // 2 - 1

                def pair_of_units(i, b, last):
                    for p in range(2):
                        number = first + b * PHEADS + 2 * i + p
                        slots(number, b, range(CHOOSE_AT))
                        if not (last and p and b == NB - 1):
                            choose(layer, number + 1, 1 - p)
                        if last and p and b == 0:
                            dve.wait_ge(match_done, PHEADS * (layer + 1) + 1)
                            zero_accumulators(1)
                        slots(number, b, range(CHOOSE_AT, SLOTS))

                for b in range(NB):
                    with dve.Fori(0, looped) as i:
                        chain.enter(i, 2 * CHOOSE_STEPS)
                        pair_of_units(i, b, False)
                    chain.leave(looped)
                    pair_of_units(looped, b, True)
                    dve.wait_ge(mm_done, (first + (b + 1) * PHEADS) * SLOTS + RING)
                    V.tensor_tensor(resid[:, b, :], psum[:, 4 * b:4 * b + 4, :].rearrange("p q n -> p (q n)"),
                                    resid[:, b, :], ALU.add).then_inc(peer_added, 1)

            norm(0)
            angles()
            latent()
            groups(mla)
            add_projection(mla)
            norm(1)
            peer(0)
            norm(2)
            forget()
            groups(fox)
            add_projection(fox)
            norm(3)
            peer(1)


_INS = ["x", "positions", "norm_mix_g", "norm_ffn_g", "mla_w_in", "mla_g_qa", "mla_w_qb", "mla_g_kva",
        "mla_w_kvb", "mla_g_q", "mla_g_k", "mla_w_o", "fox_w_in", "fox_b_f", "fox_g_q", "fox_g_k",
        "fox_w_o", "peer_w_q", "peer_sub_keys", "peer_u", "peer_v"]


def kernel(**inputs):
    import concourse.bacc as bacc
    from concourse.bass_utils import run_bass_kernel_spmd

    nc = bacc.Bacc("TRN2", target_bir_lowering=False, num_devices=1)
    arrays, args = {}, []

    def add(name, a):
        arrays[f"in_{name}_dram"] = a
        args.append(nc.dram_tensor(f"in_{name}_dram", a.shape, mybir.dt.from_np(a.dtype), kind="ExternalInput").ap())

    for name in _INS:
        add(name, np.ascontiguousarray(inputs[name]))
    exponents = np.arange(0, ROPE, 2, dtype=np.float32) / np.float32(ROPE)
    add("inv_freq", np.power(np.float32(ROPE_THETA), -exponents, dtype=np.float32)[None, :])
    out = nc.dram_tensor("out_0_dram", (1, T, D), F32, kind="ExternalOutput").ap()
    hybrid_encoder(nc, *args, out)
    r = run_bass_kernel_spmd(nc, [arrays], core_ids=[0])
    return r.results[0]["out_0_dram"]
```

```python
from contextlib import ExitStack

import numpy as np

import concourse.bass as bass
from concourse import mybir

ALU = mybir.AluOpType
ACT = mybir.ActivationFunctionType
AX_X = mybir.AxisListType.X
F32 = mybir.dt.float32
I32 = mybir.dt.int32
U32 = mybir.dt.uint32
F32R = mybir.dt.float32r

P = 128
NB = 2
T = NB * P
D = 2048
KC = D // P
TILE = 512
CHUNK = 64
EPS = 1e-6
MASKED = -1e30
LOWEST = -3.0e38

Q_RANK = KV_RANK = 512
RC = Q_RANK // P
NOPE, ROPE, VDIM = 128, 64, 128
HALF = ROPE // 2
MLA_QK = NOPE + ROPE
HEADS = 16
HD = 128
PHEADS, KEYS, TOPK = 8, 128, 16
RING = 4
SLOTS = TOPK

TWO_PI = 6.283185307179586
ROUND_MAGIC = 12582912.0
PI_A, PI_B, PI_C = 6.28125, 1.93500518798828125e-3, 3.0199159819567e-7
PI_SAFE = 3.1415925
ROPE_THETA = 10000.0
MATCH_AT = 8
CHOOSE_AT = 11
COPY_Q_AT = 4
CHOOSE_STEPS = 24


class Events:

    def __init__(self, sem, n):
        self.sem, self.n = sem, n

    def credit(self, eng):
        eng.sem_inc(self.sem, self.n)

    def at(self, turn, event):
        return (turn + 1) * self.n + event + 1

    def done(self, eng, turn, event, back=0):
        eng.wait_ge(self.sem, self.at(turn, event) - back)

    def turn_before(self, eng, turn, event=None):
        eng.wait_ge(self.sem, self.at(turn, self.n - 1 if event is None else event) - self.n)


class Chain:

    def __init__(self, eng, sem):
        self.eng, self.sem, self.base, self.n = eng, sem, 0, 0

    def step(self, ins):
        ins.then_inc(self.sem, 1)
        self.n += 1

    def settle(self):
        self.eng.wait_ge(self.sem, self.base + self.n)

    def enter(self, i, per):
        self.outer, self.per = self.base + self.n, per
        self.base, self.n = self.outer + i * per, 0

    def leave(self, turns):
        assert self.n == self.per, (self.n, self.per)
        self.base, self.n = self.outer + turns * self.per, 0


def rows_view(w):
    return w.rearrange("(k p) n -> p k n", p=P)


def hybrid_encoder(nc, x, positions, norm_mix_g, norm_ffn_g, mla_w_in, mla_g_qa, mla_w_qb, mla_g_kva,
                   mla_w_kvb, mla_g_q, mla_g_k, mla_w_o, fox_w_in, fox_b_f, fox_g_q, fox_g_k, fox_w_o,
                   peer_w_q, peer_sub_keys, peer_u, peer_v, inv_freq, out):
    with ExitStack() as ctx:
        def sb(name, shape, dt=F32):
            return ctx.enter_context(nc.sbuf_tensor(name, shape, dt))

        def sb_and_place(name, shape):
            place = (nc.sbuf_base + 31) // 32 * 32
            return sb(name, shape), place

        def parts_over(name, place, shape):
            return nc.alloc_sbuf_tensor_at(name, [P, *shape], F32R, offset=place)

        def sem(name):
            return ctx.enter_context(nc.semaphore(name))

        resid = sb("resid", [P, NB, D])
        normed, normed_at = sb_and_place("normed", [P, NB, D])
        normedT, normedT_at = sb_and_place("normedT", [P, KC, T])
        share, share_at = sb_and_place("share", [P, NB * D])
        attnT = share[:, :].rearrange("p (k t) -> p k t", k=KC)
        wbuf, wbuf_at = sb_and_place("wbuf", [P, 2, KC, TILE])
        w_low = parts_over("w_low", wbuf_at, [KC, TILE])
        w_high = parts_over("w_high", wbuf_at + 4 * KC * TILE, [KC, TILE])
        x_high = parts_over("x_high", normedT_at, [KC, T])
        other = parts_over("other", normed_at, [KC, T])
        attn_lows = parts_over("attn_lows", share_at, [KC, T])
        room = sb("room", [P, 2 * RING * D])
        u_ring = room[:, 0:RING * D].rearrange("p (r d) -> p r d", r=RING)
        v_ring = room[:, RING * D:2 * RING * D].rearrange("p (r d) -> p r d", r=RING)

        taken = [0]

        def area(n, **dims):
            a = room[:, taken[0]:taken[0] + n]
            taken[0] += n
            if dims:
                names = list(dims)
                a = a.rearrange(f"p ({' '.join(names)} rest) -> p {' '.join(names)} rest", **dims)
            return a

        gain_row = area(D)
        squares = area(NB * D, b=NB)
        taken[0] = 0
        raw_q = area(NB * TILE, b=NB)
        raw_k = area(NB * TILE, b=NB)
        raw_v = area(NB * TILE, b=NB)
        qn = area(NB * TILE, b=NB)
        kn = area(NB * TILE, b=NB)
        gate = area(NB * TILE, b=NB)
        qT = area(4 * T, h=4)
        kT = area(4 * T, h=4)
        qropeT = area(T)
        kropeT = area(T)
        masked = area(2 * T, r=2)
        probs = area(2 * T, r=2)
        probsT = area(2 * T, r=2, k=NB)
        og = area(2 * P, r=2)
        tmp_a = area(NB * 2 * ROPE, b=NB, h=2)
        tmp_b = area(NB * 2 * ROPE, b=NB, h=2)
        cqT = area(RC * T, c=RC)
        ckvT = area(RC * T, c=RC)
        taken[0] -= 2 * RC * T
        decay_rows = area(HEADS * T, h=HEADS)
        fl = area(5 * NB * HEADS, m=5, b=NB)
        decayT = area(T)
        assert taken[0] <= 2 * RING * D
        scores = share[:, 0:D]
        peer_qT = share[:, D:D + 2 * T].rearrange("p (c t) -> p c t", c=2)

        w_forget = share[:, D + 2 * T:D + 2 * T + KC * HEADS].rearrange("p (k n) -> p k n", k=KC)

        ident = sb("ident", [P, P])
        mask_mla = sb("mask_mla", [P, T])
        mask_fox = sb("mask_fox", [P, T])
        upto = sb("upto", [P, T])
        iota = sb("iota", [P, TOPK])
        inv_row = sb("inv_row", [P, HALF])
        pos_i = sb("pos_i", [P, NB], I32)
        pos_f = sb("pos_f", [P, NB])
        cos2 = sb("cos2", [P, NB, ROPE])
        sin2 = sb("sin2", [P, NB, ROPE])
        g_qa, g_kva = share[:, 0:Q_RANK], share[:, Q_RANK:Q_RANK + KV_RANK]
        keys_n = share[:, 1024:1024 + 4 * P].rearrange("p (m d) -> p m d", m=4)
        ang = share[:, 1536:1536 + 4 * T // 4].rearrange("p (m b f) -> p m b f", m=4, b=NB)
        g_cols = sb("g_cols", [P, 4])
        g_qrope = sb("g_qrope", [P, ROPE])
        g_krope = sb("g_krope", [P, ROPE])
        b_f = sb("b_f", [P, HEADS])
        k_rot = sb("k_rot", [P, NB, ROPE])
        keysT = sb("keysT", [P, 4, KEYS])
        stat = sb("stat", [P, 96])
        n_sum, n_root, n_inv = stat[:, 0:2], stat[:, 2:4], stat[:, 4:6]
        h_sum, h_root, h_inv = stat[:, 8:16], stat[:, 16:24], stat[:, 24:32]
        row_max, neg_max, row_sum, inv_sum = (stat[:, 32 + 8 * i:40 + 8 * i] for i in range(4))
        rope_sum = stat[:, 64:66]
        l_sum, l_root, l_inv = stat[:, 68:72], stat[:, 72:76], stat[:, 76:80]
        k_sum, k_root, k_inv = stat[:, 80:84], stat[:, 84:88], stat[:, 88:92]

        pick = sb("pick", [P, 2, KEYS])
        work = sb("work", [P, 2 * TOPK, TOPK])
        work_flat = work[:, :, :].rearrange("p a b -> p (a b)")
        pick_flat = pick[:, :, :].rearrange("p c n -> p (c n)")
        pick2 = work_flat[:, 0:2 * KEYS].rearrange("p (c n) -> p c n", c=2)
        cand2 = work_flat[:, 2 * KEYS:4 * KEYS]
        onehot = work
        top_s = sb("top_s", [P, 2, TOPK])
        top_i = sb("top_i", [P, 2, TOPK], U32)
        top_if = sb("top_if", [P, 2, TOPK])
        cand = sb("cand", [P, TOPK * TOPK])
        best = sb("best", [P, TOPK])
        best_pos = sb("best_pos", [P, TOPK], U32)
        pair = sb("pair", [P, 2, TOPK], U32)
        pair_f = sb("pair_f", [P, 2 * TOPK])
        key_f = sb("key_f", [P, 2 * TOPK])
        soft = sb("soft", [P, 4])
        soft_e = sb("soft_e", [P, TOPK])
        gates = sb("gates", [P, 2, TOPK])
        index = sb("index", [P, 2, TOPK], U32)
        dots = sb("dots", [P, RING])
        acts = sb("acts", [P, 2, RING])
        diag = sb("diag", [P, RING, P])

        psum = ctx.enter_context(nc.psum_tensor("psum", [P, 8, TILE], F32))

        def gbank(half, b):
            return psum[:, 2 * half + b, :]

        def sbank(r):
            return psum[:, 4 + r, :]

        def pt_bank(r):
            return psum[:, 6 + r, 0:T].rearrange("p (k t) -> p k t", k=NB)

        def o_bank(r):
            return psum[:, 6 + r, T:T + P]

        def ot_bank(r):
            return psum[:, 4 + r, T:T + P]

        consts_made = sem("consts_made")
        x_loaded = [sem(f"x_loaded{b}") for b in range(NB)]
        small_loaded = sem("small_loaded")
        gains_loaded = sem("gains_loaded")
        held = {e: sem(f"held_{e}") for e in ("pool", "dve", "act")}
        dve_steps, act_steps = sem("dve_steps"), sem("act_steps")
        w_full = [sem(f"w_full{i}") for i in range(2)]
        w_used = [sem(f"w_used{i}") for i in range(2)]
        g_full = [sem(f"g_full{i}") for i in range(2)]
        evac = [sem(f"evac{i}") for i in range(2)]
        norm_root, norm_done = sem("norm_root"), sem("norm_done")
        unit_full = [sem(f"unit_full{q}") for q in range(4)]
        unit_high, unit_low, unit_used = sem("unit_high"), sem("unit_low"), sem("unit_used")
        forget_loaded = sem("forget_loaded")
        ht_full, ht_done, ht_low = sem("ht_full"), sem("ht_done"), sem("ht_low")
        attn_high, attn_low = sem("attn_high"), sem("attn_low")
        keys_full, keys_done = sem("keys_full"), sem("keys_done")
        angles_ready, trig_ready = sem("angles_ready"), sem("trig_ready")
        lat_ss, lat_root, lat_norm, lat_full, lat_done = (
            sem(n) for n in ("lat_ss", "lat_root", "lat_norm", "lat_full", "lat_done"))
        forget_in, forget_ln, forget_log, decay_full, decay_ready = (
            sem(n) for n in ("forget_in", "forget_ln", "forget_log", "decay_full", "decay_ready"))
        o_added = sem("o_added")
        query_full, query_done, match_full, match_done = (
            sem(n) for n in ("query_full", "query_done", "match_full", "match_done"))
        first_query, first_copied, first_match = (
            sem(n) for n in ("first_query", "first_copied", "first_match"))
        acc_zero = sem("acc_zero")
        pick_ready, pick_used = sem("pick_ready"), sem("pick_used")
        best_ready, exp_ready, gate_ready, index_ready = (
            sem(n) for n in ("best_ready", "exp_ready", "gate_ready", "index_ready"))
        u_full = [sem(f"u_full{r}") for r in range(RING)]
        v_full = [sem(f"v_full{r}") for r in range(RING)]
        dot_done, diag_ready, mm_done = sem("dot_done"), sem("diag_ready"), sem("mm_done")
        peer_added = sem("peer_added")
        stored = sem("stored")

        class Attn:

            def __init__(self, layer, nh, tiles, w0, g0):
                self.layer, self.nh, self.tiles = layer, nh, tiles
                self.groups = HEADS // nh
                self.w0, self.g0 = w0, g0
                self.fox = layer == 1
                self.jobs = [(h, b) for h in range(nh) for b in range(NB)]
                nj = len(self.jobs)

                def ev(name, n):
                    return Events(sem(f"{name}{layer}"), n)

                self.ss_ready = ev("ss_ready", 2)
                self.root_ready = ev("root_ready", 2)
                self.qk_norm = ev("qk_norm", 4)
                self.t_full = ev("t_full", 4)
                self.t_done = ev("t_done", 4)
                self.s_full = ev("s_full", nj)
                self.masked = ev("masked", nj)
                self.negated = ev("negated", nj)
                self.exped = ev("exped", nj)
                self.pt_full = ev("pt_full", nj)
                self.pt_done = ev("pt_done", nj)
                self.o_full = ev("o_full", nj)
                self.og_done = ev("og_done", nj)
                self.ot_full = ev("ot_full", nj)
                self.ot_done = ev("ot_done", nj)

            def turn(self, n0, g, t):
                return (n0 + t) % 2, (n0 + t) // 2 + (self.tiles // 2) * g

            def w(self, g, t):
                return self.turn(self.w0, g, t)

            def g(self, g, t):
                return self.turn(self.g0, g, t)

        W_MLA = 0
        W_PQ0 = W_MLA + 2 * 8
        W_PQ1 = W_PQ0 + PHEADS
        S_IN = 0
        S_O0 = S_IN + 3
        S_FOX = S_O0 + 4
        S_O1 = S_FOX + 4 * 4
        G_IN = 0
        G_MLA = G_IN + 3
        G_O0 = G_MLA + 2 * 8
        G_F = G_O0 + 4
        G_FOX = G_F + 1
        G_O1 = G_FOX + 4 * 4
        S_O, W_PQ, G_O = (S_O0, S_O1), (W_PQ0, W_PQ1), (G_O0, G_O1)
        mla = Attn(0, 2, 2, W_MLA, G_MLA)
        fox = Attn(1, 4, 4, S_FOX, G_FOX)
        layers = (mla, fox)

        def psum_tile(n):
            m = n + (G_IN if n < S_O0 else G_O0 - S_O0 if n < S_FOX else G_FOX - S_FOX)
            return m % 2, m // 2

        def psum_tile_before(n, i):
            half, number = psum_tile_at(n, i)
            return 1 - half, number - 1 + half

        def psum_tile_at(n, i):
            half, number = psum_tile(n)
            return half, number + i

        def quarter(tile, q, n=TILE):
            return tile[:, 4 * q:4 * q + 4, 0:n]

        def values(q, n=TILE):
            return wbuf[:, 0, 4 * q:4 * q + 4, 0:n]

        N_CONST = 9
        N_SMALL = 13
        block = ctx.enter_context(nc.Block())

        @block.sync
        def _(sp):
            def load_tile(half, number, parts):
                sp.wait_ge(w_used[half], number + 1)
                assert len(parts) == 4
                for dst, src in parts:
                    sp.dma_start(dst, src).then_inc(w_full[half], 16)

            def quarters(half, w, cols, n):
                step = w.shape[1] // 4
                return [(wbuf[:, half, q * step:(q + 1) * step, 0:n], w[:, q * step:(q + 1) * step, cols])
                        for q in range(4)]

            def load_gains(p, g):
                sp.dma_start(gain_row, g.broadcast_to([P, D])).then_inc(gains_loaded, 16)

            for b in range(NB):
                sp.dma_start(resid[:, b, :], x[0, b * P:(b + 1) * P, :]).then_inc(x_loaded[b], 16)
            load_gains(0, norm_mix_g[0:1, :])
            def load_quarters(n, i, w, cols, width=TILE, free=False):
                for q in range(4):
                    if not free:
                        if q < 3:
                            sp.wait_ge(unit_used, 3 * (n + 2 * i - 1) + q + 1)
                        else:
                            half, number = psum_tile_before(n, i)
                            sp.wait_ge(g_full[half], 2 * number + 2)
                    sp.dma_start(values(q, width), w[:, 4 * q:4 * q + 4, cols]).then_inc(unit_full[q], 16)

            def all_used(n):
                half, number = psum_tile(n)
                sp.wait_ge(g_full[half], 2 * number + 2)

            def halves_used(n):
                for half in range(2):
                    sp.wait_ge(w_used[half], n // 2 + 1)

            def small_operands():
                count = 0
                for dst, src in (
                    (pos_i[:, 0:1], positions[0:1, 0:P].rearrange("o p -> p o")),
                    (pos_i[:, 1:2], positions[0:1, P:T].rearrange("o p -> p o")),
                    (inv_row[:, :], inv_freq.broadcast_to([P, HALF])),
                    (g_cols[:, 0:1], mla_g_q[0:1, 0:NOPE].rearrange("o p -> p o")),
                    (g_cols[:, 1:2], mla_g_k[0:1, 0:NOPE].rearrange("o p -> p o")),
                    (g_cols[:, 2:3], fox_g_q.rearrange("o p -> p o")),
                    (g_cols[:, 3:4], fox_g_k.rearrange("o p -> p o")),
                    (g_qrope[:, :], mla_g_q[0:1, NOPE:MLA_QK].broadcast_to([P, ROPE])),
                    (g_krope[:, :], mla_g_k[0:1, NOPE:MLA_QK].broadcast_to([P, ROPE])),
                    (g_qa[:, :], mla_g_qa.broadcast_to([P, Q_RANK])),
                    (g_kva[:, :], mla_g_kva.broadcast_to([P, KV_RANK])),
                    (b_f[:, :], fox_b_f.broadcast_to([P, HEADS])),
                    (keys_n[:, :, :], peer_sub_keys.rearrange("l c n d -> n (l c) d")),
                ):
                    sp.dma_start(dst, src).then_inc(small_loaded, 16)
                    count += 1
                assert count == N_SMALL

            w_in = rows_view(mla_w_in[0])
            widths = (Q_RANK, KV_RANK, ROPE)
            for t in range(3):
                c0 = sum(widths[:t])
                load_quarters(S_IN + t, 0, w_in, slice(c0, c0 + widths[t]), widths[t], free=t == 0)
                if t == 0:
                    small_operands()
            all_used(S_IN + 2)
            w_qb, w_kvb = rows_view(mla_w_qb[0]), rows_view(mla_w_kvb[0])
            with sp.Fori(0, mla.groups) as g:
                for t, (w, n) in enumerate(((w_qb, 2 * MLA_QK), (w_kvb, 2 * (NOPE + VDIM)))):
                    half, number = mla.w(g, t)
                    load_tile(half, number, quarters(half, w, bass.ds(g * n, n), n))

            def after_attention(at, g):
                w = rows_view((mla_w_o, fox_w_o)[at.layer][0])
                with sp.Fori(0, 2) as i:
                    for t in range(2):
                        load_quarters(S_O[at.layer] + t, i, w, bass.ds(i * 2 * TILE + t * TILE, TILE))
                at.ot_done.done(sp, at.groups - 1, at.ot_done.n - 1)
                load_gains(2 * at.layer + 1, g)
                all_used(S_O[at.layer] + 3)
                n0, w = W_PQ[at.layer], rows_view(peer_w_q[at.layer])
                with sp.Fori(0, PHEADS // 2) as i:
                    for t in range(2):
                        half = (n0 + t) % 2
                        load_tile(half, (n0 + t) // 2 + i,
                                  quarters(half, w, bass.ds(i * 4 * P + t * 2 * P, 2 * P), 2 * P))

            halves_used(W_PQ0)
            after_attention(mla, norm_ffn_g[0:1, :])
            halves_used(W_PQ1)
            fw = rows_view(fox_w_in[0])
            sp.dma_start(w_forget, fw[:, :, 4 * D:4 * D + HEADS]).then_inc(forget_loaded, 16)
            load_quarters(S_FOX, 0, fw, slice(0, TILE), free=True)
            sp.wait_ge(peer_added, NB)
            load_gains(2, norm_mix_g[1:2, :])
            for t in range(1, 4):
                load_quarters(S_FOX + t, 0, fw, slice(t * D, t * D + TILE))
            with sp.Fori(1, fox.groups) as g:
                for t in range(4):
                    load_quarters(S_FOX + t, 2 * g, fw, bass.ds(g * TILE + t * D, TILE))
            after_attention(fox, norm_ffn_g[1:2, :])
            for b in range(NB):
                sp.wait_ge(peer_added, NB + b + 1)
                sp.dma_start(out[0, b * P:(b + 1) * P, :], resid[:, b, :]).then_inc(stored, 16)
            sp.wait_ge(stored, 16 * NB)

        @block.gpsimd
        def _(pool):
            n = [0]

            def made(ins):
                n[0] += 1
                ins.then_inc(consts_made, 1)

            made(pool.memset(ident[:, :], 0.0))
            made(pool.memset(mask_mla[:, :], 0.0))
            made(pool.memset(mask_fox[:, :], 0.0))
            made(pool.memset(upto[:, :], 1.0))
            made(pool.iota(iota[:, :], [[1, TOPK]], base=0, channel_multiplier=0,
                           allow_small_or_imprecise_dtypes=True))
            pool.wait_ge(consts_made, n[0])
            made(pool.affine_select(out=ident[:, :], in_=ident[:, :], compare_op=ALU.not_equal, fill=1.0,
                                    base=0, pattern=[[-1, P]], channel_multiplier=1))
            made(pool.affine_select(out=mask_fox[:, P:T], in_=mask_fox[:, P:T], compare_op=ALU.is_ge,
                                    fill=MASKED, base=0, pattern=[[-1, P]], channel_multiplier=1))
            made(pool.affine_select(out=mask_mla[:, P + CHUNK:T], in_=mask_mla[:, P + CHUNK:T],
                                    compare_op=ALU.is_ge, fill=MASKED, base=-CHUNK,
                                    pattern=[[0, CHUNK]], channel_multiplier=1))
            made(pool.affine_select(out=upto[:, 0:P], in_=upto[:, 0:P], compare_op=ALU.is_ge, fill=0.0,
                                    base=0, pattern=[[1, P]], channel_multiplier=-1))
            assert n[0] == N_CONST

            def low_parts(tiles, width=TILE):
                for n in tiles:
                    for q in range(4):
                        pool.wait_ge(unit_high, 4 * n + q + 1)
                        pool.tensor_tensor(quarter(w_low, q, width), values(q, width),
                                           quarter(w_high, q, width), ALU.subtract).then_inc(unit_low, 1)

            def low_parts_looped(n0, tiles):
                with pool.Fori(0, tiles) as i:
                    low_parts([n0 + i])

            def gathers(layer, number, p):
                pool.wait_ge(index_ready, number + 1)
                for s in range(SLOTS):
                    r = s % RING
                    slot = number * SLOTS + s
                    pool.wait_ge(dot_done, slot + 1)
                    pool.sem_inc(held["pool"], 1)
                    pool.indirect_dma_start(u_ring[:, r, :], None, peer_u.rearrange("l n d -> (l n) d"),
                                            bass.IndirectOffsetOnAxis(index[:, p, s:s + 1], 0)).then_inc(u_full[r], 16)
                    pool.wait_ge(mm_done, slot + 1)
                    pool.sem_inc(held["pool"], 1)
                    pool.indirect_dma_start(v_ring[:, r, :], None, peer_v.rearrange("l n d -> (l n) d"),
                                            bass.IndirectOffsetOnAxis(index[:, p, s:s + 1], 0)).then_inc(v_full[r], 16)

            for t, width in enumerate((Q_RANK, KV_RANK, ROPE)):
                low_parts([S_IN + t], width)
            for layer in range(2):
                if layer:
                    low_parts_looped(S_FOX, 4 * fox.groups)
                low_parts_looped(S_O[layer], 4)
                with pool.Fori(0, NB * PHEADS // 2) as i:
                    for p in range(2):
                        gathers(layer, layer * NB * PHEADS + 2 * i + p, p)

        @block.tensor
        def _(pe):
            for s in (*w_used,):
                pe.sem_inc(s, 1)
            pe.sem_inc(mm_done, RING)
            pe.sem_inc(match_full, 1)

            def transpose(dst, src, k=P):
                return pe.transpose(dst, src, ident[0:k, 0:k])

            def block_transposes(p, b):
                pe.wait_ge(norm_done, 2 * p + b + 1)
                for q in range(4):
                    if b and p % 2:
                        pe.wait_ge(ht_done, 8 * p + q + 1)
                    bank = q if p % 2 else 4 * b + q
                    for c in range(4):
                        k = 4 * q + c
                        last = transpose(psum[:, bank, c * P:(c + 1) * P], normed[:, b, k * P:(k + 1) * P])
                    last.then_inc(ht_full, 1)

            def norm_transposes(p):
                for b in range(NB):
                    block_transposes(p, b)
                pe.wait_ge(ht_low, 8 * (p // 2 + 1))

            def split_gemm(n, i, width, high, low, chunks_ready=None, steps=()):
                gh, gn = psum_tile_at(n, i)
                for q in range(4):
                    pe.wait_ge(unit_low, 4 * (n + 2 * i) + q + 1)
                    if chunks_ready is not None:
                        pe.wait_ge(attn_low, chunks_ready + q + 1)
                    for b in range(NB):
                        if q == 0:
                            pe.wait_ge(evac[gh], 2 * gn + b + 1)
                        for c in range(4):
                            k = 4 * q + c
                            rows = slice(b * P, (b + 1) * P)
                            dst = gbank(gh, b)[:, 0:width]
                            pe.matmul(dst, high[:, k, rows], w_high[:, k, 0:width], start=k == 0, stop=False)
                            pe.matmul(dst, high[:, k, rows], w_low[:, k, 0:width], start=False, stop=False)
                            last = pe.matmul(dst, low[:, k, rows], w_high[:, k, 0:width],
                                             start=False, stop=k == KC - 1)
                        if q == 3:
                            last.then_inc(g_full[gh], 1)
                        elif b == NB - 1:
                            last.then_inc(unit_used, 1)
                        if steps:
                            steps.pop(0)()

            def used(wh):
                pe.sem_inc(w_used[wh], 1)

            def sub_keys():
                pe.wait_ge(small_loaded, 16 * N_SMALL)
                for m in range(4):
                    last = transpose(psum[:, 7, m * P:(m + 1) * P], keys_n[:, m, :])
                last.then_inc(keys_full, 1)

            def latent():
                for t, n in enumerate((Q_RANK, KV_RANK, ROPE)):
                    split_gemm(S_IN + t, 0, n, x_high, other)
                for t in range(2):
                    for b in range(NB):
                        pe.wait_ge(lat_norm, 2 * t + b + 1)
                        if t:
                            pe.wait_ge(lat_done, b + 1)
                        for c in range(RC):
                            last = transpose(sbank(b)[:, c * P:(c + 1) * P], (qn, kn)[t][:, b, c * P:(c + 1) * P])
                        last.then_inc(lat_full, 1)

            def forget_decay():
                gh, gn = G_F % 2, G_F // 2
                pe.wait_ge(forget_loaded, 16)
                for b in range(NB):
                    pe.wait_ge(evac[gh], 2 * gn + b + 1)
                    for k in range(KC):
                        for part in (x_high, other):
                            last = pe.matmul(gbank(gh, b)[:, 0:HEADS], part[:, k, b * P:(b + 1) * P].bitcast(F32),
                                             w_forget[:, k, :], start=k == 0 and part is x_high,
                                             stop=k == KC - 1 and part is other)
                    last.then_inc(g_full[gh], 1)
                pe.wait_ge(forget_log, 1)
                pe.matmul(psum[0:HEADS, 6, 0:T], fl[:, 4, 0, :], upto[:, :], start=True, stop=False)
                pe.matmul(psum[0:HEADS, 6, P:T], fl[:, 4, 1, :], upto[:, 0:P], start=False,
                          stop=True).then_inc(decay_full, 1)

            def qk_transposes(at, g, kind):
                src = (qn, kn)[kind]
                for b in range(NB):
                    at.qk_norm.done(pe, g, 2 * kind + b)
                    if kind == 0:
                        at.masked.turn_before(pe, g)
                        at.ot_done.turn_before(pe, g)
                    else:
                        at.t_done.done(pe, g, b)
                    for c in range(4 if at.fox else 3):
                        last = transpose(sbank(b)[:, c * P:(c + 1) * P], src[:, b, c * P:(c + 1) * P])
                    last.then_inc(at.t_full.sem, 1)

            def attention(at, g):
                nj = len(at.jobs)

                def logits(j):
                    h, b = at.jobs[j]
                    r, n = j % 2, (b + 1) * P
                    if j == 0:
                        at.t_done.done(pe, g, 3)
                    at.masked.done(pe, g, j, back=2)
                    if j >= 4:
                        at.ot_done.done(pe, g, j, back=4)
                    dst = sbank(r)[:, 0:n]
                    pe.matmul(dst, qT[:, h, b * P:(b + 1) * P], kT[:, h, 0:n], start=True, stop=False)
                    if at.fox:
                        last = pe.matmul(dst, upto[0:HEADS, P:T], decay_rows[0:HEADS, bass.ds(at.nh * g + h, 1), 0:n].rearrange("p o t -> p (o t)"),
                                         start=False, stop=True)
                    else:
                        k0 = h * ROPE
                        last = pe.matmul(dst, qropeT[k0:k0 + ROPE, b * P:(b + 1) * P],
                                         kropeT[k0:k0 + ROPE, 0:n], start=False, stop=True)
                    last.then_inc(at.s_full.sem, 1)

                def probs_transposes(j):
                    h, b = at.jobs[j]
                    at.exped.done(pe, g, j)
                    at.pt_done.done(pe, g, j, back=2)
                    at.og_done.done(pe, g, j, back=2)
                    for k in range(b + 1):
                        last = transpose(pt_bank(j % 2)[:, k, :], probs[:, j % 2, k * P:(k + 1) * P])
                    last.then_inc(at.pt_full.sem, 1)

                def values(j):
                    h, b = at.jobs[j]
                    at.pt_done.done(pe, g, j)
                    at.og_done.done(pe, g, j, back=2)
                    if j == 0:
                        for t in range(at.tiles - 2, at.tiles):
                            gh, gn = at.g(g, t)
                            pe.wait_ge(evac[gh], 2 * gn + 4)
                    for k in range(b + 1):
                        v = raw_v[:, k, h * P:(h + 1) * P] if at.fox else raw_k[:, k, (2 * h + 1) * P:(2 * h + 2) * P]
                        last = pe.matmul(o_bank(j % 2), probsT[:, j % 2, k, :], v, start=k == 0, stop=k == b)
                    last.then_inc(at.o_full.sem, 1)

                def out_transposes(j):
                    at.og_done.done(pe, g, j)
                    at.ot_done.done(pe, g, j, back=2)
                    if j + 2 < nj:
                        at.masked.done(pe, g, j + 2)
                    transpose(ot_bank(j % 2), og[:, j % 2, :]).then_inc(at.ot_full.sem, 1)

                def one(step):
                    for lag, stage in enumerate((logits, probs_transposes, values, out_transposes)):
                        if 0 <= step - lag < nj:
                            stage(step - lag)

                return [lambda step=step: one(step) for step in range(nj + 3)]

            def run(steps):
                for step in steps:
                    step()

            def mla_products(g):
                def piece(t, b, ks):
                    (wh, wn), (gh, gn) = mla.w(g, t), mla.g(g, t)
                    n = (2 * MLA_QK, 2 * (NOPE + VDIM))[t]
                    if ks[0] == 0:
                        pe.wait_ge(w_full[wh], 64 * (wn + 1))
                        pe.wait_ge(evac[gh], 2 * gn + b + 1)
                    for k in ks:
                        last = pe.matmul(gbank(gh, b)[:, 0:n], (cqT, ckvT)[t][:, k, b * P:(b + 1) * P],
                                         wbuf[:, wh, k, 0:n], start=k == 0, stop=k == RC - 1)
                    if ks[-1] == RC - 1:
                        last.then_inc(g_full[gh], 1)
                        if b == NB - 1 and t:
                            for t2 in range(2):
                                (wh, wn), (gh, gn) = mla.w(g, t2), mla.g(g, t2)
                                pe.wait_ge(g_full[gh], 2 * gn + 2)
                                pe.sem_inc(w_used[wh], 1)

                return [lambda t=t, b=b, ks=ks: piece(t, b, ks)
                        for t in range(2) for b in range(NB) for ks in (range(0, RC // 2), range(RC // 2, RC))]

            def mla_groups():
                for e in (mla.t_full, mla.s_full, mla.pt_full, mla.o_full, mla.ot_full):
                    e.credit(pe)
                pe.wait_ge(lat_done, 4)
                run(mla_products(0))
                with pe.Fori(0, mla.groups - 1) as g:
                    for kind in range(2):
                        qk_transposes(mla, g, kind)
                    steps, pieces = attention(mla, g), mla_products(g + 1)
                    for i in range(max(len(steps), len(pieces))):
                        run(steps[i:i + 1])
                        run(pieces[i:i + 1])
                for kind in range(2):
                    qk_transposes(mla, mla.groups - 1, kind)
                run(attention(mla, mla.groups - 1))

            def fox_groups():
                for e in (fox.t_full, fox.s_full, fox.pt_full, fox.o_full, fox.ot_full):
                    e.credit(pe)

                def projections(g, steps):
                    for t in range(4):
                        split_gemm(S_FOX + t, 2 * g, TILE, x_high, other, steps=steps)
                        if t in (1, 2):
                            qk_transposes(fox, g, t - 1)

                projections(0, [])
                pe.wait_ge(decay_ready, 2)
                with pe.Fori(0, fox.groups - 1) as g:
                    projections(g + 1, attention(fox, g))
                run(attention(fox, fox.groups - 1))

            def out_projection(at):
                s0 = S_O[at.layer]
                for t in range(2):
                    split_gemm(s0 + t, 0, TILE, other, attn_lows, None if t else 4 * at.layer)
                for t in range(2):
                    split_gemm(s0 + 2 + t, 0, TILE, other, attn_lows)

            def queries(layer, h, c, ks):
                wh = (W_PQ[layer] + h[1]) % 2
                head = PHEADS * layer + h[0] + h[1]
                if ks[0] == 0:
                    pe.wait_ge(w_full[wh], 64 * ((W_PQ[layer] + h[1]) // 2 + h[2] + 1))
                    pe.wait_ge(query_done, 2 * head + c + 1)
                for k in ks:
                    last = pe.matmul(psum[:, 4 + c, 0:T], wbuf[:, wh, k, c * P:(c + 1) * P],
                                     normedT[:, k, :], start=k == 0, stop=k == KC - 1)
                if ks[-1] == KC - 1:
                    last.then_inc(query_full, 1)

            def match(layer, h):
                wh = (W_PQ[layer] + h[1]) % 2
                head = PHEADS * layer + h[0] + h[1]
                pe.wait_ge(query_full, 2 * head + 2)
                used(wh)
                pe.wait_ge(query_done, 2 * head + 4)
                pe.wait_ge(match_done, head + 1)
                for b in range(NB):
                    for c in range(2):
                        last = pe.matmul(psum[:, 6 + b, c * KEYS:(c + 1) * KEYS], peer_qT[:, c, b * P:(b + 1) * P],
                                         keysT[:, 2 * layer + c, :], start=True, stop=True)
                last.then_inc(match_full, 1)

            def peer(layer):
                p, n0 = 2 * layer + 1, W_PQ[layer]

                def first_queries(b):
                    pe.wait_ge(ht_done, 8 * p + 4 * (b + 1))
                    for c in range(2):
                        for k in range(KC):
                            last = pe.matmul(psum[:, 4 + c, b * P:(b + 1) * P], wbuf[:, n0 % 2, k, c * P:(c + 1) * P],
                                             normedT[:, k, b * P:(b + 1) * P], start=k == 0, stop=k == KC - 1)
                        last.then_inc(first_query, 1)

                def first_matches(b):
                    pe.wait_ge(first_copied, 4 * layer + 2 * (b + 1))
                    for c in range(2):
                        last = pe.matmul(psum[:, 6 + b, c * KEYS:(c + 1) * KEYS], peer_qT[:, c, b * P:(b + 1) * P],
                                         keysT[:, 2 * layer + c, :], start=True, stop=True)
                    last.then_inc(match_full if b else first_match, 1)

                block_transposes(p, 0)
                pe.wait_ge(w_full[n0 % 2], 64 * (n0 // 2 + 1))
                first_queries(0)
                block_transposes(p, 1)
                first_matches(0)
                first_queries(1)
                pe.wait_ge(first_query, 4 * (layer + 1))
                used(n0 % 2)
                pe.sem_inc(query_full, 2)
                first_matches(1)

                def pair_of_units(i, b, last):
                    for p in range(2):
                        number = (NB * layer + b) * PHEADS + 2 * i + p
                        ahead = b == 0 and not (last and p)
                        head = (2 * i, p + 1, i)
                        for s in range(SLOTS):
                            r = s % RING
                            slot = number * SLOTS + s
                            pe.wait_ge(diag_ready, slot + 1 + RING)
                            pe.wait_ge(v_full[r], 16 * (number * (SLOTS // RING) + s // RING + 1))
                            for q in range(4):
                                mm = pe.matmul(psum[:, 4 * b + q, :], diag[:, r, :],
                                               v_ring[:, r, q * TILE:(q + 1) * TILE],
                                               start=False, stop=False, skip_group_check=True)
                            mm.then_inc(mm_done, 1)
                            if ahead and s < MATCH_AT:
                                queries(layer, head, s // 4, range(s % 4 * 4, s % 4 * 4 + 4))
                            if ahead and s == MATCH_AT:
                                match(layer, head)

                for b in range(NB):
                    pe.wait_ge(acc_zero, 2 * layer + b + 1)
                    with pe.Fori(0, PHEADS // 2 - 1) as i:
                        pair_of_units(i, b, False)
                    pair_of_units(PHEADS // 2 - 1, b, True)

            pe.wait_ge(consts_made, N_CONST)
            norm_transposes(0)
            sub_keys()
            latent()
            mla_groups()
            out_projection(mla)
            peer(0)
            norm_transposes(2)
            forget_decay()
            fox_groups()
            out_projection(fox)
            peer(1)

        @block.scalar
        def _(act):
            chain = Chain(act, act_steps)
            for s in evac:
                act.sem_inc(s, 2)
            act.sem_inc(query_done, 2)
            act.sem_inc(match_done, 1)
            act.sem_inc(diag_ready, RING)
            def square_root(dst, src, width, ready):
                return nc.scalar.activation(dst, src, ACT.Sqrt, bias=EPS, scale=1.0 / width).then_inc(ready, 1)

            def norm(p):
                for b in range(NB):
                    if p == 0:
                        act.wait_ge(x_loaded[b], 16)
                    elif p % 2:
                        act.wait_ge(o_added, p // 2 + 1)
                    else:
                        act.wait_ge(peer_added, NB)
                    chain.step(nc.scalar.activation(squares[:, b, :], resid[:, b, :], ACT.Square,
                                                    accum_out=n_sum[:, b:b + 1]))
                    chain.settle()
                    square_root(n_root[:, b:b + 1], n_sum[:, b:b + 1], D, norm_root)
                if p % 2:
                    return
                for b in range(NB):
                    if p == 0:
                        high_parts(S_IN, qs=(b,))
                    copy_transposed(p, b)

            def copy_transposed(p, b):
                for q in range(4):
                    act.wait_ge(ht_full, 8 * p + 4 * b + q + 1)
                    bank = q if p % 2 else 4 * b + q
                    dst = (normedT if p % 2 else x_high)[:, 4 * q:4 * q + 4, b * P:(b + 1) * P]
                    nc.scalar.activation(dst, psum[:, bank, :].rearrange("p (k t) -> p k t", k=4),
                                         ACT.Copy).then_inc(ht_done, 1)

            def high_parts(n, width=TILE, qs=range(4)):
                for q in qs:
                    act.wait_ge(unit_full[q], 16 * (n + 1))
                    nc.scalar.activation(quarter(w_high, q, width), values(q, width), ACT.Copy).then_inc(unit_high, 1)

            def out_projection(at):
                at.ot_done.done(act, at.groups - 1, at.ot_done.n - 1)
                for c in range(4):
                    nc.scalar.activation(other[:, 4 * c:4 * c + 4, :], attnT[:, 4 * c:4 * c + 4, :],
                                         ACT.Copy).then_inc(attn_high, 1)
                for t in range(1, 4):
                    high_parts(S_O[at.layer] + t)

            def copy_out(gt, b, dst, n, func=ACT.Copy):
                gh, gn = gt
                act.wait_ge(g_full[gh], 2 * gn + b + 1)
                nc.scalar.activation(dst, gbank(gh, b)[:, 0:n], func).then_inc(evac[gh], 1)

            def latent():
                tiles = ((raw_q, Q_RANK), (raw_k, KV_RANK), (raw_v, ROPE))
                for t, (dst, n) in enumerate(tiles):
                    if t < 2:
                        high_parts(S_IN + t + 1, tiles[t + 1][1], range(3))
                    for b in range(NB):
                        copy_out(((G_IN + t) % 2, (G_IN + t) // 2), b, dst[:, b, 0:n], n)
                    if t < 2:
                        high_parts(S_IN + t + 1, tiles[t + 1][1], range(3, 4))
                for t in range(2):
                    act.wait_ge(lat_ss, t + 1)
                    square_root(l_root[:, 2 * t:2 * t + 2], l_sum[:, 2 * t:2 * t + 2], Q_RANK, lat_root)
                for t in range(2):
                    for b in range(NB):
                        act.wait_ge(lat_full, 2 * t + b + 1)
                        nc.scalar.activation((cqT, ckvT)[t][:, :, b * P:(b + 1) * P],
                                             sbank(b)[:, 0:RC * P].rearrange("p (c t) -> p c t", c=RC),
                                             ACT.Copy).then_inc(lat_done, 1)

            def forget():
                act.wait_ge(forget_in, 1)
                chain.step(nc.scalar.activation(fl[:, 3], fl[:, 1], ACT.Exp, scale=-1.0))
                chain.settle()
                nc.scalar.activation(fl[:, 3], fl[:, 3], ACT.Ln, bias=1.0).then_inc(forget_ln, 1)

            def roots(at, g, kind):
                at.ss_ready.done(act, g, kind)
                root, total = ((h_root, h_sum), (k_root, k_sum))[kind] if not at.fox else (h_root, h_sum)
                n = NB * at.nh
                square_root(root[:, 0:n], total[:, 0:n], HD if at.fox else MLA_QK, at.root_ready.sem)

            def transposed(at, g, kind):
                dst = (qT, kT)[kind]
                gain = g_cols[:, 2 * at.fox + kind:2 * at.fox + kind + 1]
                if kind == 0:
                    at.s_full.turn_before(act, g)
                for b in range(NB):
                    at.t_full.done(act, g, 2 * kind + b)
                    n = at.nh
                    last = nc.scalar.activation(dst[:, 0:n, b * P:(b + 1) * P],
                                                sbank(b)[:, 0:n * P].rearrange("p (h t) -> p h t", h=n),
                                                ACT.Copy, scale=gain)
                    if not at.fox:
                        last = nc.scalar.activation((qropeT, kropeT)[kind][:, b * P:(b + 1) * P],
                                                    sbank(b)[:, n * P:(n + 1) * P], ACT.Copy)
                    last.then_inc(at.t_done.sem, 1)

            def attention_steps(at, g, between=None):
                nj = len(at.jobs)

                def exponentials(j):
                    h, b = at.jobs[j]
                    n = (b + 1) * P
                    at.negated.done(act, g, j)
                    at.pt_full.done(act, g, j, back=2)
                    nc.scalar.activation(probs[:, j % 2, 0:n], masked[:, j % 2, 0:n], ACT.Exp,
                                         bias=neg_max[:, j:j + 1],
                                         accum_out=row_sum[:, j:j + 1]).then_inc(at.exped.sem, 1)

                def probs_copy(j):
                    h, b = at.jobs[j]
                    at.pt_full.done(act, g, j)
                    at.o_full.done(act, g, j, back=2)
                    nc.scalar.activation(probsT[:, j % 2, 0:b + 1, :], pt_bank(j % 2)[:, 0:b + 1, :],
                                         ACT.Copy).then_inc(at.pt_done.sem, 1)

                def out_copy(j):
                    h, b = at.jobs[j]
                    at.ot_full.done(act, g, j)
                    act.sem_inc(held["act"], 1)
                    nc.scalar.activation(attnT[:, bass.ds(at.nh * g + h, 1), b * P:(b + 1) * P], ot_bank(j % 2).unsqueeze(1),
                                         ACT.Copy).then_inc(at.ot_done.sem, 1)

                def one(step):
                    if step < nj:
                        exponentials(step)
                    if 0 <= step - 1 < nj:
                        probs_copy(step - 1)
                    if 0 <= step - 3 < nj:
                        out_copy(step - 3)
                    if between:
                        between(step)

                return [lambda step=step: one(step) for step in range(nj + 3)]

            def attention(at, g, between=None):
                for step in attention_steps(at, g, between):
                    step()

            def mla_groups():
                for e in (mla.root_ready, mla.t_done, mla.exped, mla.pt_done, mla.ot_done):
                    e.credit(act)


                def copy_q(g):
                    for b in range(NB):
                        mla.qk_norm.turn_before(act, g, b)
                        copy_out(mla.g(g, 0), b, raw_q[:, b, 0:2 * MLA_QK], 2 * MLA_QK)

                def copy_kv(g):
                    roots(mla, g, 0)
                    mla.qk_norm.turn_before(act, g)
                    mla.o_full.turn_before(act, g)
                    for b in range(NB):
                        copy_out(mla.g(g, 1), b, raw_k[:, b, :], TILE)
                    roots(mla, g, 1)

                def both_transposed(g):
                    for kind in range(2):
                        transposed(mla, g, kind)

                copy_q(0)
                copy_kv(0)
                with act.Fori(0, mla.groups - 1) as g:
                    both_transposed(g)
                    attention(mla, g, lambda step: step == COPY_Q_AT and copy_q(g + 1))
                    copy_kv(g + 1)
                both_transposed(mla.groups - 1)
                attention(mla, mla.groups - 1, lambda step: step < 4 and high_parts(S_O0, qs=(step,)))

            def fox_groups():
                for e in (fox.root_ready, fox.t_done, fox.exped, fox.pt_done, fox.ot_done):
                    e.credit(act)

                def copy_qk(g, kind):
                    for b in range(NB):
                        fox.qk_norm.turn_before(act, g, 2 * kind + b)
                        copy_out(fox.g(g, kind), b, (raw_q, raw_k)[kind][:, b, :], TILE)

                def next_high(g, t, *qs):
                    high_parts(S_FOX + 4 * g + t + 1, qs=qs)

                def copies(g, steps):
                    def run(n, *hooks):
                        for i in range(n):
                            if steps:
                                steps.pop(0)()
                            for at_step, q in hooks:
                                if i == at_step:
                                    next_high(g, 0, q)

                    if steps:
                        run(8, (3, 0), (5, 1), (7, 2))
                    else:
                        next_high(g, 0, 0, 1, 2)
                    copy_qk(g, 0)
                    roots_now = not steps
                    if roots_now:
                        roots(fox, g, 0)
                    run(2)
                    next_high(g, 0, 3)
                    run(1)
                    if not roots_now:
                        roots(fox, g, 0)
                    next_high(g, 1, 0, 1, 2)
                    copy_qk(g, 1)
                    roots(fox, g, 1)
                    next_high(g, 1, 3)
                    transposed(fox, g, 0)
                    next_high(g, 2, 0, 1, 2)
                    fox.o_full.turn_before(act, g)
                    for b in range(NB):
                        copy_out(fox.g(g, 2), b, raw_v[:, b, :], TILE)
                    next_high(g, 2, 3)
                    transposed(fox, g, 1)
                    next_high(g, 3, 0, 1, 2)
                    fox.og_done.turn_before(act, g)
                    for b in range(NB):
                        copy_out(fox.g(g, 3), b, gate[:, b, :], TILE, ACT.Sigmoid)

                def steps_of(g):
                    return attention_steps(fox, g, lambda step: step == 0 and next_high(g, 3, 3))

                copies(0, [])
                with act.Fori(0, fox.groups - 1) as g:
                    copies(g + 1, steps_of(g))
                for step in steps_of(fox.groups - 1):
                    step()

            def peer(layer):
                first = NB * PHEADS * layer

                def copy_queries(head, c):
                    act.wait_ge(query_full, 2 * head + c + 1)
                    act.wait_ge(match_full, head + 1)
                    nc.scalar.activation(peer_qT[:, c, :], psum[:, 4 + c, 0:T], ACT.Copy).then_inc(query_done, 1)

                def copy_matches(head, number, h):
                    act.wait_ge(match_full, head + 2)
                    act.wait_ge(pick_used, number + 1)
                    nc.scalar.activation(pick_flat, psum[:, 6, 0:2 * KEYS], ACT.Copy).then_inc(pick_ready, 1)
                    nc.scalar.activation(scores[:, bass.ds(h * 2 * KEYS, 2 * KEYS)] if not isinstance(h, int) else
                                         scores[:, h * 2 * KEYS:(h + 1) * 2 * KEYS],
                                         psum[:, 7, 0:2 * KEYS], ACT.Copy).then_inc(match_done, 1)

                def fetch(number, h):
                    act.wait_ge(pick_used, number + 1)
                    act.sem_inc(held["act"], 1)
                    nc.scalar.activation(pick_flat, scores[:, bass.ds(h * 2 * KEYS, 2 * KEYS)],
                                         ACT.Copy).then_inc(pick_ready, 1)

                def soften(number):
                    act.wait_ge(best_ready, number + 1)
                    nc.scalar.activation(soft_e[:, :], best[:, :], ACT.Exp, bias=soft[:, 0:1],
                                         accum_out=soft[:, 1:2]).then_inc(exp_ready, 1)

                def slots(number, p, which):
                    for s in which:
                        r = s % RING
                        slot = number * SLOTS + s
                        act.wait_ge(dot_done, slot + 1 + RING)
                        chain.step(nc.scalar.activation(acts[:, 0, r:r + 1], dots[:, r:r + 1], ACT.Gelu))
                        chain.settle()
                        if s == 0:
                            act.wait_ge(gate_ready, number + 1)
                        chain.step(nc.scalar.activation(acts[:, 1, r:r + 1], acts[:, 0, r:r + 1], ACT.Copy,
                                                        scale=gates[:, p, s:s + 1]))
                        act.wait_ge(mm_done, slot + 1)
                        chain.settle()
                        nc.scalar.activation(diag[:, r, :], ident[:, :], ACT.Copy,
                                             scale=acts[:, 1, r:r + 1]).then_inc(diag_ready, 1)

                head = PHEADS * layer

                def copy_first_queries(b):
                    for c in range(2):
                        act.wait_ge(first_query, 4 * layer + 2 * b + c + 1)
                        nc.scalar.activation(peer_qT[:, c, b * P:(b + 1) * P], psum[:, 4 + c, b * P:(b + 1) * P],
                                             ACT.Copy).then_inc(first_copied, 1)

                copy_transposed(2 * layer + 1, 0)
                copy_first_queries(0)
                copy_transposed(2 * layer + 1, 1)
                act.wait_ge(first_match, layer + 1)
                act.wait_ge(pick_used, first + 1)
                nc.scalar.activation(pick_flat, psum[:, 6, 0:2 * KEYS], ACT.Copy).then_inc(pick_ready, 1)
                copy_first_queries(1)
                act.wait_ge(first_copied, 4 * (layer + 1))
                act.sem_inc(query_done, 2)
                act.wait_ge(match_full, head + 2)
                nc.scalar.activation(scores[:, 0:2 * KEYS], psum[:, 7, 0:2 * KEYS], ACT.Copy).then_inc(match_done, 1)
                soften(first)

                def pair_of_units(i, b, last):
                    for p in range(2):
                        h = 2 * i + p
                        number = first + b * PHEADS + h
                        ahead = b == 0 and not (last and p)
                        if ahead:
                            slots(number, p, range(0, 5))
                            copy_queries(head + h + 1, 0)
                            slots(number, p, range(5, MATCH_AT + 1))
                            copy_queries(head + h + 1, 1)
                            slots(number, p, range(MATCH_AT + 1, MATCH_AT + 2))
                            copy_matches(head + h + 1, number + 1, h + 1)
                        else:
                            if last and b and p == 0 and layer == 0:
                                high_parts(S_FOX)
                            slots(number, p, range(0, MATCH_AT + 2))
                            if b == 0:
                                fetch(number + 1, 0)
                            elif not (last and p):
                                fetch(number + 1, h + 1)
                        slots(number, p, range(MATCH_AT + 2, CHOOSE_AT))
                        if not (last and p and b == NB - 1):
                            soften(number + 1)
                        slots(number, p, range(CHOOSE_AT, SLOTS))

                looped = PHEADS // 2 - 1
                for b in range(NB):
                    with act.Fori(0, looped) as i:
                        chain.enter(i, 2 * 2 * SLOTS)
                        pair_of_units(i, b, False)
                    chain.leave(looped)
                    pair_of_units(looped, b, True)

            norm(0)
            high_parts(S_IN, qs=range(2, 4))
            act.wait_ge(keys_full, 1)
            nc.scalar.activation(keysT[:, :, :], psum[:, 7, :].rearrange("p (m n) -> p m n", m=4),
                                 ACT.Copy).then_inc(keys_done, 1)
            act.wait_ge(angles_ready, 1)
            for m in range(2):
                last = nc.scalar.activation(ang[:, 2 + m], ang[:, m], ACT.Sin)
            last.then_inc(trig_ready, 1)
            latent()
            mla_groups()
            out_projection(mla)
            norm(1)
            peer(0)
            norm(2)
            forget()
            fox_groups()
            out_projection(fox)
            norm(3)
            peer(1)

        @block.vector
        def _(dve):
            V = nc.vector
            chain = Chain(dve, dve_steps)

            def step(ins):
                chain.step(ins)

            def hold():
                dve.sem_inc(held["dve"], 1)

            dve.sem_inc(dot_done, RING)
            dve.sem_inc(pick_used, 1)

            def angles():
                dve.wait_ge(small_loaded, 16 * N_SMALL)
                dve.wait_ge(consts_made, N_CONST)
                step(V.tensor_copy(pos_f[:, :], pos_i[:, :]))
                chain.settle()
                for b in range(NB):
                    step(V.tensor_scalar(ang[:, 0, b, :], inv_row[:, :], pos_f[:, b:b + 1], None, ALU.mult))
                chain.settle()
                step(V.tensor_scalar(ang[:, 1], ang[:, 0], 1.0 / TWO_PI, ROUND_MAGIC, ALU.mult, ALU.add))
                chain.settle()
                step(V.tensor_scalar(ang[:, 1], ang[:, 1], ROUND_MAGIC, None, ALU.subtract))
                for part in (PI_A, PI_B, PI_C):
                    chain.settle()
                    step(V.scalar_tensor_tensor(out=ang[:, 0], in0=ang[:, 1], scalar=-part, in1=ang[:, 0],
                                                op0=ALU.mult, op1=ALU.add))
                chain.settle()
                step(V.tensor_scalar(ang[:, 0], ang[:, 0], PI_SAFE, -PI_SAFE, ALU.min, ALU.max))
                chain.settle()
                step(V.scalar_tensor_tensor(out=ang[:, 1], in0=ang[:, 0], scalar=-1.0, in1=ang[:, 0],
                                            op0=ALU.mult, op1=ALU.max))
                chain.settle()
                V.tensor_scalar(ang[:, 1], ang[:, 1], -1.0, TWO_PI / 4, ALU.mult, ALU.add).then_inc(angles_ready, 1)
                step(V.tensor_scalar(g_cols[:, 0:1], g_cols[:, 0:1], MLA_QK ** -0.5, None, ALU.mult))
                step(V.tensor_scalar(g_cols[:, 2:3], g_cols[:, 2:3], HD ** -0.5, None, ALU.mult))
                step(V.tensor_scalar(g_qrope[:, :], g_qrope[:, :], MLA_QK ** -0.5, None, ALU.mult))
                dve.wait_ge(trig_ready, 1)
                step(V.tensor_scalar(sin2[:, :, 0:HALF], ang[:, 2], -1.0, None, ALU.mult))
                step(V.tensor_copy(sin2[:, :, HALF:ROPE], ang[:, 2]))
                step(V.tensor_copy(cos2[:, :, 0:HALF], ang[:, 3]))
                step(V.tensor_copy(cos2[:, :, HALF:ROPE], ang[:, 3]))
                chain.settle()

            def norm(p):
                for b in range(NB):
                    dve.wait_ge(norm_root, 2 * p + b + 1)
                    step(V.reciprocal(n_inv[:, b:b + 1], n_root[:, b:b + 1]))
                    chain.settle()
                    dve.wait_ge(gains_loaded, 16 * (p + 1))
                    V.scalar_tensor_tensor(out=normed[:, b, :], in0=resid[:, b, :], scalar=n_inv[:, b:b + 1],
                                           in1=gain_row, op0=ALU.mult, op1=ALU.mult).then_inc(norm_done, 1)
                if p % 2 == 0:
                    dve.wait_ge(ht_full, 8 * (p + 1))
                    for b in range(NB):
                        for q in range(4):
                            dve.wait_ge(ht_done, 8 * p + 4 * b + q + 1)
                            chunks, rows = slice(4 * q, 4 * q + 4), slice(b * P, (b + 1) * P)
                            V.tensor_tensor(other[:, chunks, rows],
                                            psum[:, 4 * b + q, :].rearrange("p (k t) -> p k t", k=4),
                                            x_high[:, chunks, rows], ALU.subtract).then_inc(ht_low, 1)

            def sum_squares(src, junk, dst):
                return V.tensor_tensor_reduce(junk, src, src, 1.0, 0.0, ALU.mult, ALU.add, dst)

            def rotate(dst, src, b, heads, ta, tb):
                def over_heads(a):
                    return a.unsqueeze(1).broadcast_to([P, heads, a.shape[-1]])
                step(V.tensor_tensor(ta, src, over_heads(cos2[:, b, :]), ALU.mult))
                step(V.tensor_tensor(tb[:, :, 0:HALF], src[:, :, HALF:ROPE], over_heads(sin2[:, b, 0:HALF]), ALU.mult))
                step(V.tensor_tensor(tb[:, :, HALF:ROPE], src[:, :, 0:HALF], over_heads(sin2[:, b, HALF:ROPE]), ALU.mult))
                chain.settle()
                return V.tensor_tensor(dst, ta, tb, ALU.add)

            def latent():
                for t, raw in enumerate((raw_q, raw_k)):
                    for b in range(NB):
                        dve.wait_ge(evac[(G_IN + t) % 2], 2 * ((G_IN + t) // 2) + b + 3)
                        last = sum_squares(raw[:, b, :], (qn, kn)[t][:, b, :], l_sum[:, 2 * t + b:2 * t + b + 1])
                    last.then_inc(lat_ss, 1)
                for t, (raw, g) in enumerate(((raw_q, g_qa), (raw_k, g_kva))):
                    dve.wait_ge(lat_root, t + 1)
                    step(V.reciprocal(l_inv[:, 2 * t:2 * t + 2], l_root[:, 2 * t:2 * t + 2]))
                    chain.settle()
                    for b in range(NB):
                        V.scalar_tensor_tensor(out=(qn, kn)[t][:, b, :], in0=raw[:, b, :],
                                               scalar=l_inv[:, 2 * t + b:2 * t + b + 1], in1=g[:, :],
                                               op0=ALU.mult, op1=ALU.mult).then_inc(lat_norm, 1)
                for b in range(NB):
                    dve.wait_ge(evac[(G_IN + 2) % 2], 2 * ((G_IN + 2) // 2) + b + 3)
                    kr = raw_v[:, b, 0:ROPE]
                    step(sum_squares(kr, tmp_a[:, b, 1, :], rope_sum[:, b:b + 1]))
                    chain.settle()
                    step(V.tensor_tensor(raw_v[:, b, ROPE:2 * ROPE], kr, g_krope[:, :], ALU.mult))
                    chain.settle()
                    step(rotate(k_rot[:, b:b + 1, :], raw_v[:, b:b + 1, ROPE:2 * ROPE], b, 1,
                                tmp_a[:, b, 0:1, :], tmp_b[:, b, 0:1, :]))
                chain.settle()

            def forget():
                gh, gn = G_F % 2, G_F // 2
                for b in range(NB):
                    dve.wait_ge(g_full[gh], 2 * gn + b + 1)
                    V.tensor_tensor(fl[:, 0, b, :], gbank(gh, b)[:, 0:HEADS], b_f[:, :], ALU.add).then_inc(evac[gh], 1)
                dve.wait_ge(evac[gh], 2 * gn + 4)
                step(V.tensor_scalar(fl[:, 2], fl[:, 0], 0.0, None, ALU.min))
                V.scalar_tensor_tensor(out=fl[:, 1], in0=fl[:, 0], scalar=-1.0, in1=fl[:, 0],
                                       op0=ALU.mult, op1=ALU.max).then_inc(forget_in, 1)
                dve.wait_ge(forget_ln, 1)
                chain.settle()
                V.tensor_tensor(fl[:, 4], fl[:, 2], fl[:, 3], ALU.subtract).then_inc(forget_log, 1)
                dve.wait_ge(decay_full, 1)
                V.tensor_copy(decayT[0:HEADS, :], psum[0:HEADS, 6, 0:T]).then_inc(decay_ready, 1)
                dve.wait_ge(decay_ready, 1)
                V.scalar_tensor_tensor(out=decay_rows[0:HEADS, :, :],
                                       in0=decayT[0:HEADS, :].unsqueeze(1).broadcast_to([HEADS, HEADS, T]),
                                       scalar=-1.0,
                                       in1=ident[0:HEADS, 0:HEADS].unsqueeze(2).broadcast_to([HEADS, HEADS, T]),
                                       op0=ALU.mult, op1=ALU.mult).then_inc(decay_ready, 1)

            def head_norms(at, g, kind, part=None):
                raw, dst = ((raw_q, qn), (raw_k, kn))[kind]
                total, root, inv = ((h_sum, h_root, h_inv), (k_sum, k_root, k_inv))[kind] if not at.fox else (
                    h_sum, h_root, h_inv)
                nh = at.nh
                gh, gn = at.g(g, kind)
                for b in range(NB if part != 1 else 0):
                    dve.wait_ge(evac[gh], 2 * gn + b + 3)
                    at.t_full.turn_before(dve, g, 2 * kind + b)
                    for h in range(nh):
                        if at.fox:
                            src = raw[:, b, h * P:(h + 1) * P]
                        elif kind == 0:
                            src = raw[:, b, h * MLA_QK:(h + 1) * MLA_QK]
                        else:
                            src = raw[:, b, 2 * h * P:(2 * h + 1) * P]
                        last = sum_squares(src, dst[:, b, h * src.shape[-1]:(h + 1) * src.shape[-1]], total[:, b * nh + h:b * nh + h + 1])
                        if not at.fox and kind:
                            step(last)
                if not at.fox and kind and part != 1:
                    chain.settle()
                    last = V.tensor_tensor(total[:, 0:2 * nh].rearrange("p (b h) -> p b h", b=NB),
                                           total[:, 0:2 * nh].rearrange("p (b h) -> p b h", b=NB),
                                           rope_sum.unsqueeze(2).broadcast_to([P, NB, nh]), ALU.add)
                if part != 1:
                    last.then_inc(at.ss_ready.sem, 1)
                if part == 0:
                    return
                at.root_ready.done(dve, g, kind)
                step(V.reciprocal(inv[:, 0:2 * nh], root[:, 0:2 * nh]))
                chain.settle()
                for b in range(NB):
                    def per_head(n):
                        return inv[:, b * nh:(b + 1) * nh].unsqueeze(2).broadcast_to([P, nh, n])
                    if at.fox:
                        V.tensor_tensor(dst[:, b, :].rearrange("p (h d) -> p h d", h=nh),
                                        raw[:, b, :].rearrange("p (h d) -> p h d", h=nh), per_head(P),
                                        ALU.mult).then_inc(at.qk_norm.sem, 1)
                        continue
                    nope = dst[:, b, 0:nh * P].rearrange("p (h d) -> p h d", h=nh)
                    rope = dst[:, b, nh * P:nh * P + nh * ROPE].rearrange("p (h d) -> p h d", h=nh)
                    if kind == 0:
                        src = raw[:, b, 0:nh * MLA_QK].rearrange("p (h d) -> p h d", h=nh)
                        step(V.tensor_tensor(nope, src[:, :, 0:NOPE], per_head(NOPE), ALU.mult))
                        step(V.tensor_tensor(rope, src[:, :, NOPE:MLA_QK], per_head(ROPE), ALU.mult))
                        chain.settle()
                        step(V.tensor_tensor(rope, rope, g_qrope[:, :].unsqueeze(1).broadcast_to([P, nh, ROPE]), ALU.mult))
                        chain.settle()
                        rotate(rope, rope, b, nh, tmp_a[:, b], tmp_b[:, b]).then_inc(at.qk_norm.sem, 1)
                    else:
                        src = raw[:, b, :].rearrange("p (h d) -> p h d", h=nh)
                        step(V.tensor_tensor(nope, src[:, :, 0:NOPE], per_head(NOPE), ALU.mult))
                        V.tensor_tensor(rope, k_rot[:, b, :].unsqueeze(1).broadcast_to([P, nh, ROPE]),
                                        per_head(ROPE), ALU.mult).then_inc(at.qk_norm.sem, 1)

            def attention(at, g, between=None):
                nj = len(at.jobs)
                mask = mask_fox if at.fox else mask_mla

                def mask_and_max(j):
                    h, b = at.jobs[j]
                    n = (b + 1) * P
                    at.s_full.done(dve, g, j)
                    at.exped.done(dve, g, j, back=2)
                    hold()
                    V.tensor_tensor_reduce(masked[:, j % 2, 0:n], sbank(j % 2)[:, 0:n], mask[:, T - n:T], 1.0,
                                           LOWEST, ALU.add, ALU.max, row_max[:, j:j + 1]).then_inc(at.masked.sem, 1)
                    at.masked.done(dve, g, j)
                    V.tensor_scalar(neg_max[:, j:j + 1], row_max[:, j:j + 1], -1.0, None,
                                    ALU.mult).then_inc(at.negated.sem, 1)

                def finish(j):
                    h, b = at.jobs[j]
                    at.exped.done(dve, g, j)
                    step(V.reciprocal(inv_sum[:, j:j + 1], row_sum[:, j:j + 1]))
                    at.o_full.done(dve, g, j)
                    at.ot_full.done(dve, g, j, back=2)
                    chain.settle()
                    if at.fox:
                        if j == 0:
                            gh, gn = at.g(g, 3)
                            dve.wait_ge(evac[gh], 2 * gn + 4)
                        last = V.scalar_tensor_tensor(out=og[:, j % 2, :], in0=o_bank(j % 2),
                                                      scalar=inv_sum[:, j:j + 1], in1=gate[:, b, h * P:(h + 1) * P],
                                                      op0=ALU.mult, op1=ALU.mult)
                    else:
                        last = V.tensor_scalar(og[:, j % 2, :], o_bank(j % 2), inv_sum[:, j:j + 1], None, ALU.mult)
                    last.then_inc(at.og_done.sem, 1)

                for s in range(nj + 2):
                    if s < nj:
                        mask_and_max(s)
                    if s >= 2:
                        finish(s - 2)
                    if between:
                        between(s)

            def groups(at):
                for e in (at.ss_ready, at.qk_norm, at.masked, at.negated, at.og_done):
                    e.credit(dve)
                nj = len(at.jobs)
                per = 2 + nj if at.fox else 2 + nj + 4 + NB * (3 + 3) + NB
                for kind in range(2):
                    head_norms(at, 0, kind)
                with dve.Fori(0, at.groups - 1) as g:
                    chain.enter(g, per)
                    if at.fox:
                        attention(at, g)
                        head_norms(at, g + 1, 0)
                    else:
                        attention(at, g, lambda s: s == COPY_Q_AT and head_norms(at, g + 1, 0, part=0))
                        head_norms(at, g + 1, 0, part=1)
                    head_norms(at, g + 1, 1)
                chain.leave(at.groups - 1)
                attention(at, at.groups - 1)

            def add_projection(at):
                for c in range(4):
                    dve.wait_ge(attn_high, 4 * at.layer + c + 1)
                    chunks = slice(4 * c, 4 * c + 4)
                    V.tensor_tensor(attn_lows[:, chunks, :], attnT[:, chunks, :],
                                    other[:, chunks, :], ALU.subtract).then_inc(attn_low, 1)
                g0 = G_O[at.layer]
                with dve.Fori(0, 2) as i:
                    for t in range(2):
                        gh, gn = (g0 + t) % 2, (g0 + t) // 2 + i
                        for b in range(NB):
                            dve.wait_ge(g_full[gh], 2 * gn + b + 1)
                            cols = resid[:, b, bass.ds(i * 2 * TILE + t * TILE, TILE)]
                            V.tensor_tensor(cols, gbank(gh, b), cols, ALU.add).then_inc(evac[gh], 1)
                for t in range(2):
                    dve.wait_ge(evac[(g0 + t) % 2], 2 * ((g0 + t) // 2 + 1) + 4)
                dve.sem_inc(o_added, 1)

            def choose(layer, number, p):
                dve.wait_ge(pick_ready, number + 1)
                hold()
                for c in range(2):
                    step(V.max(top_s[:, c, 0:8], pick[:, c, :]))
                chain.settle()
                hold()
                for c in range(2):
                    step(V.max_index(top_i[:, c, 0:8], top_s[:, c, 0:8], pick[:, c, :]))
                    last = V.match_replace(pick2[:, c, :], top_s[:, c, 0:8], pick[:, c, :], LOWEST)
                    if c:
                        last.then_inc(pick_used, 1)
                    else:
                        step(last)
                chain.settle()
                dve.wait_ge(pick_used, number + 2)
                hold()
                for c in range(2):
                    step(V.max(top_s[:, c, 8:16], pick2[:, c, :]))
                chain.settle()
                hold()
                for c in range(2):
                    step(V.max_index(top_i[:, c, 8:16], top_s[:, c, 8:16], pick2[:, c, :]))
                step(V.tensor_tensor(cand[:, :].rearrange("p (i j) -> p i j", i=TOPK),
                                     top_s[:, 0, :].unsqueeze(2).broadcast_to([P, TOPK, TOPK]),
                                     top_s[:, 1, :].unsqueeze(1).broadcast_to([P, TOPK, TOPK]), ALU.add))
                chain.settle()
                step(V.tensor_scalar(top_if[:, 0, :], top_i[:, 0, :], float(KEYS), None, ALU.mult))
                step(V.tensor_scalar(top_if[:, 1, :], top_i[:, 1, :], float(layer * KEYS * KEYS), None, ALU.add))
                step(V.max(best[:, 0:8], cand[:, :]))
                chain.settle()
                hold()
                step(V.max_index(best_pos[:, 0:8], best[:, 0:8], cand[:, :]))
                step(V.match_replace(cand2[:, :], best[:, 0:8], cand[:, :], LOWEST))
                chain.settle()
                hold()
                step(V.max(best[:, 8:16], cand2[:, :]))
                chain.settle()
                V.tensor_scalar(soft[:, 0:1], best[:, 0:1], -1.0, None, ALU.mult).then_inc(best_ready, 1)
                step(V.max_index(best_pos[:, 8:16], best[:, 8:16], cand2[:, :]))
                chain.settle()
                step(V.tensor_scalar(pair[:, 0, :], best_pos[:, :], 4, None, ALU.logical_shift_right))
                step(V.tensor_scalar(pair[:, 1, :], best_pos[:, :], TOPK - 1, None, ALU.bitwise_and))
                chain.settle()
                step(V.tensor_copy(pair_f[:, :], pair[:, :, :].rearrange("p c k -> p (c k)")))
                chain.settle()
                step(V.tensor_tensor(onehot[:, :, :], pair_f[:, :].unsqueeze(2).broadcast_to([P, 2 * TOPK, TOPK]),
                                     iota[:, :].unsqueeze(1).broadcast_to([P, 2 * TOPK, TOPK]), ALU.is_equal))
                chain.settle()
                hot = onehot[:, :, :].rearrange("p (c k) n -> p c k n", c=2)
                step(V.tensor_tensor(hot, hot, top_if[:, :, :].unsqueeze(2).broadcast_to([P, 2, TOPK, TOPK]), ALU.mult))
                chain.settle()
                step(V.tensor_reduce(key_f[:, :], onehot[:, :, :], AX_X, ALU.add))
                chain.settle()
                if not isinstance(number, int) or number > 0:
                    dve.wait_ge(mm_done, (number - 1) * SLOTS + RING)
                V.tensor_tensor(index[:, p, :], key_f[:, 0:TOPK], key_f[:, TOPK:2 * TOPK],
                                ALU.add).then_inc(index_ready, 1)
                dve.wait_ge(exp_ready, number + 1)
                step(V.reciprocal(soft[:, 2:3], soft[:, 1:2]))
                chain.settle()
                V.tensor_scalar(gates[:, p, :], soft_e[:, :], soft[:, 2:3], None, ALU.mult).then_inc(gate_ready, 1)

            def slots(number, b, which):
                for s in which:
                    r = s % RING
                    slot = number * SLOTS + s
                    dve.wait_ge(u_full[r], 16 * (number * (SLOTS // RING) + s // RING + 1))
                    dve.wait_ge(diag_ready, slot + 1)
                    V.tensor_tensor_reduce(u_ring[:, r, :], u_ring[:, r, :], normed[:, b, :], 1.0, 0.0,
                                           ALU.mult, ALU.add, dots[:, r:r + 1]).then_inc(dot_done, 1)

            def zero_accumulators(b):
                V.memset(psum[:, 4 * b:4 * b + 4, :], 0.0).then_inc(acc_zero, 1)

            def peer(layer):
                first = NB * PHEADS * layer
                choose(layer, first, 0)
                dve.wait_ge(ht_done, 8 * (2 * layer + 2))
                zero_accumulators(0)
                looped = PHEADS // 2 - 1

                def pair_of_units(i, b, last):
                    for p in range(2):
                        number = first + b * PHEADS + 2 * i + p
                        slots(number, b, range(CHOOSE_AT))
                        if not (last and p and b == NB - 1):
                            choose(layer, number + 1, 1 - p)
                        if last and p and b == 0:
                            dve.wait_ge(match_done, PHEADS * (layer + 1) + 1)
                            zero_accumulators(1)
                        slots(number, b, range(CHOOSE_AT, SLOTS))

                for b in range(NB):
                    with dve.Fori(0, looped) as i:
                        chain.enter(i, 2 * CHOOSE_STEPS)
                        pair_of_units(i, b, False)
                    chain.leave(looped)
                    pair_of_units(looped, b, True)
                    dve.wait_ge(mm_done, (first + (b + 1) * PHEADS) * SLOTS + RING)
                    V.tensor_tensor(resid[:, b, :], psum[:, 4 * b:4 * b + 4, :].rearrange("p q n -> p (q n)"),
                                    resid[:, b, :], ALU.add).then_inc(peer_added, 1)

            norm(0)
            angles()
            latent()
            groups(mla)
            add_projection(mla)
            norm(1)
            peer(0)
            norm(2)
            forget()
            groups(fox)
            add_projection(fox)
            norm(3)
            peer(1)


_INS = ["x", "positions", "norm_mix_g", "norm_ffn_g", "mla_w_in", "mla_g_qa", "mla_w_qb", "mla_g_kva",
        "mla_w_kvb", "mla_g_q", "mla_g_k", "mla_w_o", "fox_w_in", "fox_b_f", "fox_g_q", "fox_g_k",
        "fox_w_o", "peer_w_q", "peer_sub_keys", "peer_u", "peer_v"]


def kernel(**inputs):
    import concourse.bacc as bacc
    from concourse.bass_utils import run_bass_kernel_spmd

    nc = bacc.Bacc("TRN2", target_bir_lowering=False, num_devices=1)
    arrays, args = {}, []

    def add(name, a):
        arrays[f"in_{name}_dram"] = a
        args.append(nc.dram_tensor(f"in_{name}_dram", a.shape, mybir.dt.from_np(a.dtype), kind="ExternalInput").ap())

    for name in _INS:
        add(name, np.ascontiguousarray(inputs[name]))
    exponents = np.arange(0, ROPE, 2, dtype=np.float32) / np.float32(ROPE)
    add("inv_freq", np.power(np.float32(ROPE_THETA), -exponents, dtype=np.float32)[None, :])
    out = nc.dram_tensor("out_0_dram", (1, T, D), F32, kind="ExternalOutput").ap()
    hybrid_encoder(nc, *args, out)
    r = run_bass_kernel_spmd(nc, [arrays], core_ids=[0])
    return r.results[0]["out_0_dram"]
```
